# Optimizing a Trainium2 kernel written in Bass

```python
import math
import jax, jax.numpy as jnp
from jax import lax
import numpy as np

D_MODEL = 1024
BATCH = 1
SEQ = 256
DEPTH = 2

N_MIXERS = 2
N_GLA_LAYERS = (DEPTH + 1) // 2
N_ATTN_LAYERS = DEPTH // 2

GRID_W = 64

GLA_HEADS = 4
GLA_KEY_DIM = D_MODEL // 2
GLA_VAL_DIM = D_MODEL
GLA_DK = GLA_KEY_DIM // GLA_HEADS
GLA_DV = GLA_VAL_DIM // GLA_HEADS
GLA_GATE_RANK = 16
GLA_GATE_NORMALIZER = 16.0
GLA_CHUNK = 64
GLA_IN_DIM = 2 * GLA_KEY_DIM + 2 * GLA_VAL_DIM + 2 * GLA_GATE_RANK

ATTN_HEAD_DIM = 128
ATTN_Q_HEADS = D_MODEL // ATTN_HEAD_DIM
ATTN_KV_HEADS = 2
ATTN_GROUP = ATTN_Q_HEADS // ATTN_KV_HEADS
ATTN_QKV_DIM = (ATTN_Q_HEADS + 2 * ATTN_KV_HEADS) * ATTN_HEAD_DIM
QUERY_BLOCK = 128
ROPE_THETA = 10000.0
ROPE_PAIRS_PER_AXIS = ATTN_HEAD_DIM // 4

D_FF = 2816
CONV_WIDTH = 3

NORM_EPS = 1e-6


def rmsnorm(x, w):
    xf = x.astype(jnp.float32)
    y = xf * lax.rsqrt(jnp.mean(xf * xf, axis=-1, keepdims=True) + NORM_EPS)
    return (y * w.astype(jnp.float32)).astype(x.dtype)

def gla_chunked(q, k, v, log_a, strict):
    B, H, S, dk = q.shape
    dv = v.shape[-1]
    n = S // GLA_CHUNK
    c = lambda t: t.reshape(B, H, n, GLA_CHUNK, t.shape[-1])
    q, k, v, log_a = c(q), c(k), c(v), c(log_a)
    b = jnp.cumsum(log_a, axis=3)
    b_end = b[:, :, :, -1:, :]
    q_dec = q * jnp.exp(b)
    k_inv = k * jnp.exp(-b)
    mask = jnp.tril(jnp.ones((GLA_CHUNK, GLA_CHUNK), dtype=bool), k=-1 if strict else 0)
    att = jnp.where(mask, jnp.einsum('bhncd,bhnsd->bhncs', q_dec, k_inv), 0.0)
    o_intra = jnp.einsum('bhncs,bhnsv->bhncv', att, v)
    kv_chunk = jnp.einsum('bhncd,bhncv->bhndv', k * jnp.exp(b_end - b), v)
    decay_chunk = jnp.exp(b_end[:, :, :, 0, :])

    def step(state, inp):
        d, kv_c = inp
        return d[..., None] * state + kv_c, state

    _, s_prev = lax.scan(step, jnp.zeros((B, H, dk, dv), jnp.float32),
                         (jnp.moveaxis(decay_chunk, 2, 0), jnp.moveaxis(kv_chunk, 2, 0)))
    s_prev = jnp.moveaxis(s_prev, 0, 2)
    o_inter = jnp.einsum('bhncd,bhndv->bhncv', q_dec, s_prev)
    return (o_intra + o_inter).reshape(B, H, S, dv)

def gla_mixer(h, w_in, w_gate_up_f, b_gate_f, w_gate_up_b, b_gate_b, norm_w, w_out):
    B, S, _ = h.shape
    f32 = jnp.float32
    proj = h @ w_in
    q, k, v, g, r = jnp.split(
        proj, [GLA_KEY_DIM, 2 * GLA_KEY_DIM, 2 * GLA_KEY_DIM + GLA_VAL_DIM,
               2 * GLA_KEY_DIM + 2 * GLA_VAL_DIM], axis=-1)
    r_f, r_b = jnp.split(r, 2, axis=-1)

    def heads(t, d):
        return t.reshape(B, S, GLA_HEADS, d).transpose(0, 2, 1, 3).astype(f32)

    def log_decay(r_dir, w_up, b_up):
        logits = (r_dir @ w_up + b_up).astype(f32)
        return heads(jax.nn.log_sigmoid(logits) / GLA_GATE_NORMALIZER, GLA_DK)

    q = heads(q, GLA_DK) * (GLA_DK ** -0.5)
    k = heads(k, GLA_DK)
    v = heads(v, GLA_DV)
    la_f = log_decay(r_f, w_gate_up_f, b_gate_f)
    la_b = log_decay(r_b, w_gate_up_b, b_gate_b)
    flip = lambda t: jnp.flip(t, axis=2)
    o_f = gla_chunked(q, k, v, la_f, strict=False)
    o_b = flip(gla_chunked(flip(q), flip(k), flip(v), flip(la_b), strict=True))
    o = (o_f + o_b).transpose(0, 2, 1, 3)
    o = rmsnorm(o, norm_w) * jax.nn.silu(g.astype(f32).reshape(B, S, GLA_HEADS, GLA_DV))
    return o.reshape(B, S, GLA_VAL_DIM).astype(h.dtype) @ w_out

def apply_rope(x, cos, sin):
    half = x.shape[-1] // 2
    x1, x2 = x[..., :half], x[..., half:]
    return jnp.concatenate([x1 * cos - x2 * sin, x1 * sin + x2 * cos], axis=-1)

def attn_mixer(h, w_qkv, q_norm, k_norm, w_out, cos, sin):
    B, S, _ = h.shape
    proj = h @ w_qkv
    q, k, v = jnp.split(proj, [ATTN_Q_HEADS * ATTN_HEAD_DIM,
                               (ATTN_Q_HEADS + ATTN_KV_HEADS) * ATTN_HEAD_DIM], axis=-1)
    q = q.reshape(B, S, ATTN_Q_HEADS, ATTN_HEAD_DIM)
    k = k.reshape(B, S, ATTN_KV_HEADS, ATTN_HEAD_DIM)
    v = v.reshape(B, S, ATTN_KV_HEADS, ATTN_HEAD_DIM)
    q = apply_rope(rmsnorm(q, q_norm).astype(jnp.float32), cos, sin).astype(h.dtype)
    k = apply_rope(rmsnorm(k, k_norm).astype(jnp.float32), cos, sin).astype(h.dtype)
    n_blk = S // QUERY_BLOCK
    qb = q.reshape(B, S, ATTN_KV_HEADS, ATTN_GROUP, ATTN_HEAD_DIM).transpose(0, 2, 3, 1, 4)
    qb = qb.reshape(B, ATTN_KV_HEADS, ATTN_GROUP, n_blk, QUERY_BLOCK, ATTN_HEAD_DIM)
    qb = qb.transpose(3, 0, 1, 2, 4, 5)
    k = k.transpose(0, 2, 1, 3)
    v = v.transpose(0, 2, 1, 3)
    scale = ATTN_HEAD_DIM ** -0.5

    def block(q_blk):
        s = jnp.einsum('bkgqd,bksd->bkgqs', q_blk, k).astype(jnp.float32) * scale
        p = jax.nn.softmax(s, axis=-1).astype(v.dtype)
        return jnp.einsum('bkgqs,bksd->bkgqd', p, v)

    o = lax.map(block, qb)
    o = o.transpose(1, 0, 4, 2, 3, 5).reshape(B, S, ATTN_Q_HEADS * ATTN_HEAD_DIM)
    return o @ w_out

def conv_ffn(h, w_up, w_conv, b_conv, w_down):
    u = h @ w_up
    u = lax.conv_general_dilated(
        u, w_conv[:, None, :], window_strides=(1,), padding=[(1, 1)],
        dimension_numbers=('NWC', 'WIO', 'NWC'), feature_group_count=u.shape[-1]) + b_conv
    val, gate = jnp.split(u, 2, axis=-1)
    return (jax.nn.silu(gate) * val) @ w_down

def first_inputs(seed: int = 0) -> dict:
    key = jax.random.key(seed)
    ks = jax.random.split(key, 20)
    nrm = lambda k, shape, s: jax.random.normal(k, shape, jnp.float32) * s
    NG, NA = N_GLA_LAYERS, N_ATTN_LAYERS
    return {
        'x': nrm(ks[0], (BATCH, SEQ, D_MODEL), 1.0),
        'norm_mix': 1.0 + nrm(ks[1], (DEPTH, D_MODEL), 0.01),
        'norm_ffn': 1.0 + nrm(ks[2], (DEPTH, D_MODEL), 0.01),
        'gla_w_in': nrm(ks[3], (NG, D_MODEL, GLA_IN_DIM), D_MODEL ** -0.5),
        'gla_w_gate_up_f': nrm(ks[4], (NG, GLA_GATE_RANK, GLA_KEY_DIM), GLA_GATE_RANK ** -0.5),
        'gla_b_gate_f': nrm(ks[5], (NG, GLA_KEY_DIM), 0.1),
        'gla_w_gate_up_b': nrm(ks[6], (NG, GLA_GATE_RANK, GLA_KEY_DIM), GLA_GATE_RANK ** -0.5),
        'gla_b_gate_b': nrm(ks[7], (NG, GLA_KEY_DIM), 0.1),
        'gla_norm': 1.0 + nrm(ks[8], (NG, GLA_DV), 0.01),
        'gla_w_out': nrm(ks[9], (NG, GLA_VAL_DIM, D_MODEL), GLA_VAL_DIM ** -0.5),
        'attn_w_qkv': nrm(ks[10], (NA, D_MODEL, ATTN_QKV_DIM), D_MODEL ** -0.5),
        'attn_q_norm': 1.0 + nrm(ks[11], (NA, ATTN_HEAD_DIM), 0.01),
        'attn_k_norm': 1.0 + nrm(ks[12], (NA, ATTN_HEAD_DIM), 0.01),
        'attn_w_out': nrm(ks[13], (NA, ATTN_Q_HEADS * ATTN_HEAD_DIM, D_MODEL),
                          (ATTN_Q_HEADS * ATTN_HEAD_DIM) ** -0.5),
        'ffn_w_up': nrm(ks[14], (DEPTH, D_MODEL, 2 * D_FF), D_MODEL ** -0.5),
        'ffn_w_conv': nrm(ks[15], (DEPTH, CONV_WIDTH, 2 * D_FF), CONV_WIDTH ** -0.5),
        'ffn_b_conv': nrm(ks[16], (DEPTH, 2 * D_FF), 0.01),
        'ffn_w_down': nrm(ks[17], (DEPTH, D_FF, D_MODEL), D_FF ** -0.5),
    }

def first_block(x, norm_mix, norm_ffn, gla_w_in, gla_w_gate_up_f, gla_b_gate_f,
              gla_w_gate_up_b, gla_b_gate_b, gla_norm, gla_w_out,
              attn_w_qkv, attn_q_norm, attn_k_norm, attn_w_out,
              ffn_w_up, ffn_w_conv, ffn_b_conv, ffn_w_down):
    S = x.shape[1]
    rows = S // GRID_W
    f32 = jnp.float32
    row_idx = jnp.repeat(jnp.arange(rows, dtype=f32), GRID_W)
    col_idx = jnp.tile(jnp.arange(GRID_W, dtype=f32), rows)
    inv_freq = ROPE_THETA ** (-jnp.arange(ROPE_PAIRS_PER_AXIS, dtype=f32) / ROPE_PAIRS_PER_AXIS)
    ang = jnp.concatenate([row_idx[:, None] * inv_freq, col_idx[:, None] * inv_freq], axis=-1)
    cos = jnp.cos(ang)[None, :, None, :]
    sin = jnp.sin(ang)[None, :, None, :]

    for i in range(DEPTH):
        h = rmsnorm(x, norm_mix[i])
        j = i // N_MIXERS
        if i % N_MIXERS == 0:
            x = x + gla_mixer(h, gla_w_in[j], gla_w_gate_up_f[j], gla_b_gate_f[j],
                              gla_w_gate_up_b[j], gla_b_gate_b[j], gla_norm[j], gla_w_out[j])
        else:
            x = x + attn_mixer(h, attn_w_qkv[j], attn_q_norm[j], attn_k_norm[j],
                               attn_w_out[j], cos, sin)
        x = x + conv_ffn(rmsnorm(x, norm_ffn[i]), ffn_w_up[i], ffn_w_conv[i],
                         ffn_b_conv[i], ffn_w_down[i])
    return x


N_A = (DEPTH + 1) // 2
N_B = DEPTH // 2
WIDTH = 3 * D_MODEL // 2
LRU_HEADS = 12
LRU_BLOCK = WIDTH // LRU_HEADS
CONV_A = 4
CONV_B = 3
LRU_C = 8.0


def rmsnorm_2(x, g):
    xf = x.astype(jnp.float32)
    inv = lax.rsqrt(jnp.mean(xf * xf, axis=-1, keepdims=True) + NORM_EPS)
    return (xf * inv * g.astype(jnp.float32)).astype(x.dtype)

def causal_depthwise_conv(u, w, b=None):
    k_width = w.shape[0]
    s = u.shape[1]
    up = jnp.pad(u, ((0, 0), (k_width - 1, 0), (0, 0)))
    out = up[:, 0:s] * w[0]
    for k in range(1, k_width):
        out = out + up[:, k:k + s] * w[k]
    if b is not None:
        out = out + b
    return out

def rg_lru(u, gate_w, gate_b, lam):
    bsz, s, w = u.shape
    uh = u.reshape(bsz, s, LRU_HEADS, LRU_BLOCK)
    g = jnp.einsum('bshi,hio->bsho', uh, gate_w) + gate_b
    g = jax.nn.sigmoid(g.astype(jnp.float32))
    r = g[..., :LRU_BLOCK].reshape(bsz, s, w)
    i = g[..., LRU_BLOCK:].reshape(bsz, s, w)
    log_a = -LRU_C * r * jax.nn.softplus(-lam.astype(jnp.float32))
    a = jnp.exp(log_a)
    mult = jnp.sqrt(-jnp.expm1(2.0 * log_a))
    bterm = mult * (i * u.astype(jnp.float32))

    def combine(left, right):
        a_l, b_l = left
        a_r, b_r = right
        return a_l * a_r, a_r * b_l + b_r

    _, h = lax.associative_scan(combine, (a, bterm), axis=1)
    return h.astype(u.dtype)

def recurrent_mixer(h, w_in, conv_w, conv_b, gate_w, gate_b, lam, w_out):
    u = jnp.einsum('bsd,dc->bsc', h, w_in)
    gate, xb = u[..., :WIDTH], u[..., WIDTH:]
    xb = causal_depthwise_conv(xb, conv_w, conv_b)
    y = rg_lru(xb, gate_w, gate_b, lam)
    return jnp.einsum('bsc,cd->bsd', y * jax.nn.silu(gate), w_out)

def shortconv_mixer(h, w_in, conv_w, w_out):
    u = jnp.einsum('bsd,dc->bsc', h, w_in)
    bg = u[..., :WIDTH]
    cg = u[..., WIDTH:2 * WIDTH]
    xv = u[..., 2 * WIDTH:3 * WIDTH]
    gate = u[..., 3 * WIDTH:]
    y = bg * causal_depthwise_conv(cg * xv, conv_w)
    return jnp.einsum('bsc,cd->bsd', y * jax.nn.silu(gate), w_out)

def second_inputs(seed: int = 0) -> dict:
    key = jax.random.key(seed)
    ks = jax.random.split(key, 16)
    f32 = jnp.float32
    x = jax.random.normal(ks[0], (BATCH, SEQ, D_MODEL), f32)
    norm_g = 1.0 + 0.02 * jax.random.normal(ks[1], (DEPTH, D_MODEL), f32)
    a_w_in = jax.random.normal(ks[2], (N_A, D_MODEL, 2 * WIDTH), f32) * D_MODEL ** -0.5
    a_conv_w = jax.random.normal(ks[3], (N_A, CONV_A, WIDTH), f32) * CONV_A ** -0.5
    a_conv_b = 0.02 * jax.random.normal(ks[4], (N_A, WIDTH), f32)
    a_gate_w = jax.random.normal(ks[5], (N_A, LRU_HEADS, LRU_BLOCK, 2 * LRU_BLOCK), f32) * LRU_BLOCK ** -0.5
    a_gate_b = 0.02 * jax.random.normal(ks[6], (N_A, LRU_HEADS, 2 * LRU_BLOCK), f32)
    a0 = jax.random.uniform(ks[7], (N_A, WIDTH), f32, minval=0.9, maxval=0.999)
    a_lambda = jnp.log(a0) - jnp.log1p(-a0)
    a_w_out = jax.random.normal(ks[8], (N_A, WIDTH, D_MODEL), f32) * WIDTH ** -0.5
    b_w_in = jax.random.normal(ks[9], (N_B, D_MODEL, 4 * WIDTH), f32) * D_MODEL ** -0.5
    b_conv_w = jax.random.normal(ks[10], (N_B, CONV_B, WIDTH), f32) * CONV_B ** -0.5
    b_w_out = jax.random.normal(ks[11], (N_B, WIDTH, D_MODEL), f32) * WIDTH ** -0.5
    final_g = 1.0 + 0.02 * jax.random.normal(ks[12], (D_MODEL,), f32)
    return {"x": x, "norm_g": norm_g, "a_w_in": a_w_in, "a_conv_w": a_conv_w,
            "a_conv_b": a_conv_b, "a_gate_w": a_gate_w, "a_gate_b": a_gate_b,
            "a_lambda": a_lambda, "a_w_out": a_w_out, "b_w_in": b_w_in,
            "b_conv_w": b_conv_w, "b_w_out": b_w_out, "final_g": final_g}

def second_block(x, norm_g, a_w_in, a_conv_w, a_conv_b, a_gate_w, a_gate_b, a_lambda,
              a_w_out, b_w_in, b_conv_w, b_w_out, final_g):
    for i in range(DEPTH):
        h = rmsnorm_2(x, norm_g[i])
        j = i // N_MIXERS
        if i % N_MIXERS == 0:
            x = x + recurrent_mixer(h, a_w_in[j], a_conv_w[j], a_conv_b[j], a_gate_w[j],
                                    a_gate_b[j], a_lambda[j], a_w_out[j])
        else:
            x = x + shortconv_mixer(h, b_w_in[j], b_conv_w[j], b_w_out[j])
    return rmsnorm_2(x, final_g)


def setup_inputs(seed=0):
    out = dict(first_inputs(seed))
    for name, value in second_inputs(seed + 1).items():
        if name != "x":
            out[name + "_2"] = value
    return out


def reference(
    x, norm_mix, norm_ffn, gla_w_in, gla_w_gate_up_f, gla_b_gate_f, gla_w_gate_up_b,
    gla_b_gate_b, gla_norm, gla_w_out, attn_w_qkv, attn_q_norm, attn_k_norm, attn_w_out,
    ffn_w_up, ffn_w_conv, ffn_b_conv, ffn_w_down, norm_g_2, a_w_in_2, a_conv_w_2, a_conv_b_2,
    a_gate_w_2, a_gate_b_2, a_lambda_2, a_w_out_2, b_w_in_2, b_conv_w_2, b_w_out_2, final_g_2,
):
    x = first_block(
        x, norm_mix, norm_ffn, gla_w_in, gla_w_gate_up_f, gla_b_gate_f, gla_w_gate_up_b,
        gla_b_gate_b, gla_norm, gla_w_out, attn_w_qkv, attn_q_norm, attn_k_norm, attn_w_out,
        ffn_w_up, ffn_w_conv, ffn_b_conv, ffn_w_down,
    )
    return second_block(
        x, norm_g_2, a_w_in_2, a_conv_w_2, a_conv_b_2, a_gate_w_2, a_gate_b_2, a_lambda_2,
        a_w_out_2, b_w_in_2, b_conv_w_2, b_w_out_2, final_g_2,
    )


_drawn_inputs = setup_inputs


def setup_inputs(seed=0):
    import zlib

    import numpy as np

    out = dict(_drawn_inputs(seed))
    spreads = {}
    factors = {'norm_mix': 3.498,
     'norm_ffn': 4.679,
     'gla_norm': 7.648,
     'attn_q_norm': 8.0,
     'attn_k_norm': 8.0,
     'ffn_b_conv': 4.774,
     'norm_g_2': 3.184,
     'a_conv_b_2': 9.587,
     'a_gate_b_2': 33.029,
     'final_g_2': 8.026}
    for name, (base, spread) in spreads.items():
        noise = np.random.default_rng([zlib.crc32(name.encode()), seed]).standard_normal(out[name].shape)
        drawn = base * np.exp(spread * noise) if base else spread * noise
        out[name] = __import__('jax').numpy.asarray(drawn.astype(out[name].dtype))
    for name, factor in factors.items():
        out[name] = (out[name] * factor).astype(out[name].dtype)
    return out
```

```python
import math
from contextlib import ExitStack

import numpy as np

import concourse.bass as bass
from concourse import mybir

P = 128
D = 1024
S = 256
T = S // P
KC = D // P
EPS = 1e-6
GLA_HEADS, GLA_DK, GLA_DV, GLA_RANK, CHUNK = 4, 128, 256, 16, 64
GLA_KEYS = GLA_HEADS * GLA_DK
GATE_NORM = 16.0
Q_HEADS, KV_HEADS, HD = 8, 2, 128
GROUP = Q_HEADS // KV_HEADS
D_FF = 2816
WIDTH = 1536
LRU_HEADS = WIDTH // P
LRU_C = 8.0

UNIT = 2048
RAW = 3
RING = 6
FFN_ITERS = D_FF // 256
LRU_ITERS = LRU_HEADS // 2
SC_ITERS = WIDTH // P
U_Q, U_K, U_V, U_G, U_GO = 0, 2, 4, 8, 12
U_FFN = [16, 59]
FFN_UNITS = 3 * FFN_ITERS
U_KV = U_FFN[0] + FFN_UNITS
U_AQ, U_AO = U_KV + 2, U_KV + 6
assert U_AO + 4 == U_FFN[1]
U_LRU = U_FFN[1] + FFN_UNITS
U_SC = U_LRU + 3 * LRU_ITERS
UNITS = U_SC + 3 * SC_ITERS


def sc_half(u):
    n = u - U_SC
    return n == 3 * SC_ITERS - 1 or (n >= 2 and (n - 2) % 3 == 2)


NORMS = ["mix0", "ffn0", "mix1", "ffn1", "lru", "sc"]
C_GAMMA = {n: KC * i for i, n in enumerate(NORMS)}
C_FFN = [KC * len(NORMS) + i * 8 * D_FF // P for i in range(2)]
C_GB = C_FFN[1] + 8 * D_FF // P
C_LCONV = C_GB + 2 * GLA_HEADS
C_LGB = C_LCONV + 5 * LRU_HEADS
C_LAM = C_LGB + 2 * LRU_HEADS
C_SCONV = C_LAM + LRU_HEADS
N_PAR = C_SCONV + 3 * SC_ITERS
R_FINAL, R_GLA, R_QN, R_KN = 0, D, D + GLA_DV, D + GLA_DV + HD
N_ROW = R_KN + HD

def generations():
    g, f, first, full = 0, 0, {}, {}
    stages = [("norm_mix0", 4, 4), ("rank", 1, 1), ("q", 2, 0), ("k", 2, 0), ("z", 4, 4),
              ("att", 2 * GLA_HEADS, 2 * GLA_HEADS), ("o", 0, 1), ("turn", 4, 4),
              ("norm_ffn0", 4, 4), ("ffn0", 2 * FFN_ITERS, 0),
              ("norm_mix1", 4, 4), ("kv", 2, 0), ("kT", 1, 1), ("qT", 4, 4),
              ("heads", 3 * Q_HEADS, 3 * Q_HEADS),
              ("norm_ffn1", 4, 4), ("ffn1", 2 * FFN_ITERS, 0),
              ("norm_lru", 4, 4), ("lru", 0, 2 * LRU_ITERS),
              ("norm_sc", 4, 4), ("sc", 2 * SC_ITERS, 0)]
    for name, banks, signals in stages:
        first[name], full[name] = g, f + 1
        g, f = g + banks, f + signals
    return first, full


GEN, FULL = generations()


def head_gens():
    order, n = {}, 0
    for h in range(Q_HEADS + 2):
        for kind, head in (("s", h), ("p", h - 1), ("o", h - 2)):
            if 0 <= head < Q_HEADS:
                order[kind, head] = n
                n += 1
    return order


def lru_plan():
    units, u = {}, U_LRU
    for j in range(LRU_ITERS + 2):
        for kind, e in (("x", j), ("g", j), ("d", j - 2)):
            if 0 <= e < LRU_ITERS:
                units[kind, e] = u
                u += 1
    assert u == U_SC
    return units


def up_unit(base, e, k):
    return base + k if e == 0 else base + 3 * e - 1 + k


HEAD_AT = head_gens()
LRU_UNIT = lru_plan()
BRANCH_BANK, GATE_BANK, HEAD_BANK = 0, 1, 2
LRU_AHEAD = [[97, 98, 99], [100, 101], [102, 103, 104], [105, 106, 107], [108, 109, 110], [111, 112, 113]]
LRU_AHEAD = [[U_LRU - 92 + u for u in step] for step in LRU_AHEAD]

FREED = {"ffn0": 1, "mix1": 2, "ao": 3, "ffn1": 4, "lru": 5, "sc": 6, "final": 7}
XN = {"mix0": 0, "gla": 2, "ffn0": 4, "mix1": 6, "ffn1": 8, "lru": 10, "sc": 12}
HH = {"mix0": 0, "turn": 4, "ffn0": 8, "mix1": 12, "heads": 16, "ffn1": 24, "lru": 28, "sc": 32}
N_CONSTS = 5
STEP_FFN = [0, FFN_ITERS]
STEP_LRU = 2 * FFN_ITERS
STEP_SC = STEP_LRU + LRU_ITERS
RMS = {"mix0": 0, "gla": 2, "ffn0": 4, "mix1": 6, "k": 8, "q": 9, "ffn1": 11, "lru": 13, "sc": 15, "final": 17}
SUMS = {"mix0": 0, "gla": 2, "ffn0": 4, "mix1": 6, "ffn1": 8, "lru": 10, "sc": 12, "final": 14}


class Chain:

    def __init__(self, eng, sem):
        self.eng, self.sem, self.n, self.per, self.i = eng, sem, 0, 0, 0

    def mark(self, ins):
        ins.then_inc(self.sem, 1)
        self.n += 1

    def wait(self):
        self.eng.wait_ge(self.sem, self.n + self.per * self.i)

    def enter(self, per, i):
        self.per, self.i, self.start = per, i, self.n

    def leave(self, trips):
        assert self.n - self.start == self.per, (self.n - self.start, self.per)
        self.n, self.per, self.i = self.start + self.per * trips, 0, 0


def two_block_kernel(nc, x_in, stream, par_in, row_in, wr_in, gup_in, gatew_in, rope_in, out):
    f32, f32r, u32 = mybir.dt.float32, mybir.dt.float32r, mybir.dt.uint32
    ALU, ACT, AX = mybir.AluOpType, mybir.ActivationFunctionType, mybir.AxisListType

    ctx = ExitStack()
    with ctx:
        def sem(name):
            return ctx.enter_context(nc.semaphore(name))

        top = (nc.sbuf_base + 63) // 64 * 64

        def put(name, shape, dt=f32, at=None):
            nonlocal top
            offset = top if at is None else at
            if at is None:
                top += (4 * int(np.prod(shape[1:])) + 31) // 32 * 32
            return nc.alloc_sbuf_tensor_at(name, shape, dt, offset=offset)

        raw = put("raw", [P, RAW, UNIT])
        w_hi = put("w_hi", [P, RING, UNIT], f32r)
        w_lo = put("w_lo", [P, RING, UNIT], f32r)
        x = put("x", [P, T, D])
        h_at = top
        h_hi = put("h_hi", [P, KC, S], f32r)
        h_lo = put("h_lo", [P, KC, S], f32r)
        par = put("par", [P, N_PAR])
        row = put("row", [P, N_ROW])
        wr = put("wr", [P, KC, 2 * GLA_RANK])
        gup = put("gup", [GLA_RANK, 2, GLA_KEYS])
        rope = put("rope", [P, T, 2, HD])
        ident = put("ident", [P, P])
        causal = put("causal", [P, T, P])
        chunk_on = put("chunk_on", [P, S])
        zeros = put("zeros", [P, 512], f32r)
        power = put("power", [P, 20])
        rt = put("rt", [GLA_RANK, 2, S])
        stat, mean, rstd = (put(n, [P, 20]) for n in ("stat", "mean", "rstd"))
        sp4, lam_e, lam_s, lam_q, lam_p = (put(n, [P, LRU_HEADS]) for n in ("sp4", "lam_e", "lam_s", "lam_q", "lam_p"))
        xn_at = top
        xn = put("xn", [P, T, D])
        a_hi = put("a_hi", [P, 2, 2, S], f32r)
        a_lo = put("a_lo", [P, 2, 2, S], f32r)
        stage_at = top
        gatew_at = nc.sbuf_usable_end // 64 * 64 - 4 * LRU_HEADS * 2 * P
        gatew = put("gatew", [P, LRU_HEADS, 2 * P], at=gatew_at)

        def stage(at, end, *buffers):
            made = []
            for name, shape in buffers:
                made.append(put(name, shape, at=at))
                at += (4 * int(np.prod(shape[1:])) + 31) // 32 * 32
            assert at <= end, (buffers[0][0], at - end)
            return made

        sbuf_end = nc.sbuf_usable_end
        v, qT, kT, la = stage(stage_at, sbuf_end, ("v", [P, T, D]), ("qT", [P, GLA_HEADS, S]),
                              ("kT", [P, GLA_HEADS, S]), ("la", [P, 2, GLA_HEADS, S]))
        lt, = stage(xn_at, stage_at, ("lt", [P, 2, GLA_HEADS, S]))
        ep, en, ed, dd, qd, ki, kd, qt, kt = stage(
            xn_at, stage_at, *((n, [P, 2, S]) for n in ("ep", "en", "ed", "dd", "qd", "ki", "kd")),
            ("qt", [P, 2, P]), ("kt", [P, 2, P]))
        att_c, att_x = stage(h_at, h_at + 4 * KC * S, ("att_c", [P, 2, T, P]), ("att_x", [P, 2, T, P]))
        sg = put("sg", [P, T, D], at=h_at + 4 * KC * S)
        cacc, sgl, actf = stage(stage_at, gatew_at, ("cacc", [P, 2, 2, S]), ("sgl", [P, 2, S]), ("actf", [P, 2, S]))
        qn, qr, kv, kr, kT2 = stage(
            stage_at, sbuf_end, ("qn", [P, T, D]), ("qr", [P, T, D]), ("kv", [P, T, 2 * KV_HEADS * HD]),
            ("kr", [P, T, KV_HEADS * HD]), ("kT2", [P, KV_HEADS, S]))
        qT2 = put("qT2", [P, Q_HEADS, S], at=stage_at)
        rtmp, tabs, nb, sm, mx = stage(xn_at + 4 * D, stage_at, ("rtmp", [P, D]), ("tabs", [P, 2, 2, T, HD]),
                                   ("nb", [P, 2, T]), ("sm", [P, 2, T]), ("mx", [P, 2, T]))
        sq = put("sq", [P, D], at=xn_at)
        pt = put("pt", [P, 2, T, S], at=xn_at)
        kn = put("kn", [P, T, KV_HEADS * HD], at=xn_at + 4 * D + 2 * D)
        pm = put("pm", [P, 2, T, S], at=xn_at + 4 * D)
        xc, gg, rg, ig, ug, iu = stage(stage_at, gatew_at, *((n, [P, 2, S]) for n in ("xc", "gg", "rg", "ig", "ug", "iu")))
        rr, sgate, su = stage(xn_at, xn_at + 4 * T * D, *((n, [P, 2, S]) for n in ("rr", "sgate", "su")))
        p1, aa, yy, actl = rg, ig, su, rr
        cgs, pp, ct, sgs, ys, acts = stage(stage_at, gatew_at, *((n, [P, S]) for n in ("cgs", "pp", "ct", "sgs", "ys", "acts")))

        ring = ctx.enter_context(nc.psum_tensor("ring", [P, 4, 512], f32))
        acc = ctx.enter_context(nc.psum_tensor("acc", [P, T, D], f32))

        x_loaded, consts_loaded, gatew_loaded = sem("x_loaded"), sem("consts_loaded"), sem("gatew_loaded")
        raw_loaded = [sem(f"raw_loaded{s}") for s in range(RAW)]
        hi_split = sem("hi_split")
        lo_split = sem("lo_split")
        used = sem("used")
        filled = sem("filled")
        ring_free = sem("ring_free")
        acc_free = [sem(f"acc_free{t}") for t in range(T)]
        sumsq = sem("sumsq")
        head_sumsq = sem("head_sumsq")
        rms_ready = sem("rms_ready")
        xn_ready = sem("xn_ready")
        h_hi_ready = sem("h_hi_ready")
        made = sem("made")
        tables_ready = sem("tables_ready")
        z_abs, soft_ready, scan_ready = sem("z_abs"), sem("soft_ready"), sem("scan_ready")
        dd_ready, exps_ready, prod_ready = sem("dd_ready"), sem("exps_ready"), sem("prod_ready")
        v_ready, sg_ready = sem("v_ready"), sem("sg_ready")
        taps_ready = sem("taps_ready")
        gate_ready = sem("gate_ready")
        act_ready = sem("act_ready")
        a_hi_ready, a_lo_ready = sem("a_hi_ready"), sem("a_lo_ready")
        sq_ready, roped = sem("sq_ready"), sem("roped")
        nb_ready, exp_ready = sem("nb_ready"), sem("exp_ready")
        lam_ready, sp4_ready = sem("lam_ready"), sem("sp4_ready")
        ri_ready, tanh_ready, sqrt_ready = sem("ri_ready"), sem("tanh_ready"), sem("sqrt_ready")
        cg_ready = sem("cg_ready")
        branch_free, gate_free, heads_free = sem("branch_free"), sem("gate_free"), sem("heads_free")
        out_ready, out_stored = sem("out_ready"), sem("out_stored")
        act_own, dve_own, pool_own = sem("act_own"), sem("dve_own"), sem("pool_own")

        block = ctx.enter_context(nc.Block())

        @block.sync
        def _(sp):
            def load(u, i=0, half=False):
                n = UNIT // 2 if half else UNIT
                src = stream[bass.ds(u + 3 * i, 1), :, 0:n].rearrange("o p n -> (o p) n")
                sp.dma_start(raw[:, u % RAW, 0:n], src).then_inc(raw_loaded[u % RAW], 16)

            sp.dma_start(x[:, :, :], x_in.rearrange("o (t p) d -> p (o t) d", p=P)).then_inc(x_loaded, 16)
            for u in range(RAW):
                load(u)
            whole = (U_SC + 2 - RAW) // RAW
            with sp.Fori(0, whole) as i:
                for k in range(RAW):
                    sp.wait_ge(lo_split, RAW * i + k + 1)
                    load(RAW + k, i)
            for u in range(RAW + RAW * whole, U_SC + 2):
                sp.wait_ge(lo_split, u - RAW + 1)
                load(u)
            with sp.Fori(0, SC_ITERS - 1) as i:
                for k in range(RAW):
                    sp.wait_ge(lo_split, RAW * i + U_SC + 2 + k - RAW + 1)
                    load(U_SC + 2 + k, i, half=k == 2)
            sp.wait_ge(lo_split, UNITS - RAW)
            load(UNITS - 1, half=True)
            for t in range(T):
                sp.wait_ge(out_ready, t + 1)
                sp.dma_start(out[0, t * P:(t + 1) * P, :], xn[:, t, :]).then_inc(out_stored, 16)
            sp.wait_ge(out_stored, 16 * T)

        @block.gpsimd
        def _(pool):
            own = Chain(pool, pool_own)
            own.mark(nc.gpsimd.memset(power[:, :], -0.5))
            nc.gpsimd.memset(zeros[:, :].bitcast(f32), 0.0).then_inc(made, 1)
            for b in (ident, causal, chunk_on):
                own.mark(nc.gpsimd.memset(b[:, :] if b is not causal else b[:, :, :], 1.0))
            own.wait()
            nc.gpsimd.affine_select(out=ident[:, :], in_=ident[:, :], compare_op=ALU.is_equal, fill=0.0,
                                    base=0, pattern=[[-1, P]], channel_multiplier=1).then_inc(made, 1)
            nc.gpsimd.affine_select(out=causal[:, :, :], in_=causal[:, :, :], compare_op=ALU.is_ge, fill=0.0,
                                    base=0, pattern=[[0, T], [1, P]], channel_multiplier=-1).then_inc(made, 1)
            nc.gpsimd.affine_select(out=chunk_on[:, :].rearrange("p (c n) -> p c n", n=CHUNK),
                                    in_=chunk_on[:, :].rearrange("p (c n) -> p c n", n=CHUNK),
                                    compare_op=ALU.is_gt, fill=0.0, base=0,
                                    pattern=[[0, S // CHUNK], [1, CHUNK]], channel_multiplier=0).then_inc(made, 1)

            def rms(first, n, width):
                own.mark(nc.gpsimd.tensor_scalar(mean[:, first:first + n], stat[:, first:first + n],
                                                 1.0 / width, EPS, ALU.mult, ALU.add))
                own.wait()
                nc.gpsimd.tensor_tensor(rstd[:, first:first + n], mean[:, first:first + n],
                                        power[:, first:first + n], ALU.pow).then_inc(rms_ready, 1)

            def rms_of_x(name):
                for t in range(T):
                    pool.wait_ge(sumsq, SUMS[name] + t + 1)
                    rms(t, 1, D)

            rms_of_x("mix0")
            for t in range(T):
                pool.wait_ge(sumsq, SUMS["gla"] + t + 1)
                rms(GLA_HEADS * t, GLA_HEADS, GLA_DV)
            rms_of_x("ffn0")
            rms_of_x("mix1")
            pool.wait_ge(filled, FULL["norm_mix1"] + 3)
            for n, r in ((0, R_QN), (1, R_KN)):
                def weight(a, m):
                    return row[:, a:a + m].unsqueeze(1).to_broadcast([P, T, m])
                half = HD // 2
                nc.gpsimd.tensor_tensor(tabs[:, n, 0, :, :], rope[:, :, 0, :], weight(r, HD), ALU.mult).then_inc(tables_ready, 1)
                nc.gpsimd.tensor_tensor(tabs[:, n, 1, :, 0:half], rope[:, :, 1, 0:half], weight(r + half, half),
                                        ALU.mult).then_inc(tables_ready, 1)
                nc.gpsimd.tensor_tensor(tabs[:, n, 1, :, half:HD], rope[:, :, 1, half:HD], weight(r, half),
                                        ALU.mult).then_inc(tables_ready, 1)
            pool.wait_ge(head_sumsq, 1)
            rms(16, T * KV_HEADS, HD)
            for t in range(T):
                pool.wait_ge(head_sumsq, t + 2)
                rms(Q_HEADS * t, Q_HEADS, HD)
            rms_of_x("ffn1")
            pool.dma_start(gatew[:, :, :], gatew_in.rearrange("p (h n) -> p h n", h=LRU_HEADS)).then_inc(gatew_loaded, 16)
            for name in ("lru", "sc", "final"):
                rms_of_x(name)

        @block.scalar
        def _(act):
            own = Chain(act, act_own)

            def split(u, i=0, half=False):
                n = UNIT // 2 if half else UNIT
                act.wait_ge(raw_loaded[u % RAW], 16 * (u // RAW + 1) + 16 * (RING // RAW) * i)
                if u >= RING:
                    act.wait_ge(used, u - RING + 1 + RING * i)
                nc.scalar.activation(w_hi[:, u % RING, 0:n], raw[:, u % RAW, 0:n], ACT.Copy).then_inc(hi_split, 1)

            def sums(t, name):
                if name != "mix0":
                    act.wait_ge(acc_free[t], FREED[name])
                nc.scalar.activation(xn[:, t, :], x[:, t, :], ACT.Square, accum_out=stat[:, t:t + 1]).then_inc(sumsq, 1)

            def turned(name):
                for b in range(4):
                    act.wait_ge(filled, FULL["norm_" + name] + b)
                    for k in range(2):
                        kc = 2 * b + k
                        last = nc.scalar.activation(h_hi[:, kc, :], ring[:, (GEN["norm_" + name] + b) % 4, k * S:(k + 1) * S],
                                                    ACT.Copy, scale=par[:, C_GAMMA[name] + kc:C_GAMMA[name] + kc + 1])
                    last.then_inc(h_hi_ready, 1)

            act.dma_start(par[:, :], par_in).then_inc(consts_loaded, 16)
            act.dma_start(wr[:, :, :], wr_in.rearrange("p (c n) -> p c n", c=KC)).then_inc(consts_loaded, 16)
            act.dma_start(gup[:, :, :], gup_in.rearrange("r (a n) -> r a n", a=2)).then_inc(consts_loaded, 16)
            act.dma_start(row[:, :], row_in.partition_broadcast(P)).then_inc(consts_loaded, 16)
            act.dma_start(rope[:, :, :, :], rope_in.rearrange("p (t a n) -> p t a n", t=T, a=2)).then_inc(consts_loaded, 16)
            act.wait_ge(x_loaded, 16)
            for t in range(T):
                sums(t, "mix0")
            split(0)
            split(1)
            act.wait_ge(consts_loaded, 16 * N_CONSTS)
            turned("mix0")
            own.mark(nc.scalar.activation(lam_p[:, :], par[:, C_LAM:C_LAM + LRU_HEADS], ACT.Abs))
            own.wait()
            nc.scalar.activation(lam_e[:, :], lam_p[:, :], ACT.Exp, scale=-1.0).then_inc(lam_ready, 1)
            for u in range(2, 6):
                split(u)
            for d in range(2):
                for b in range(2):
                    g = GEN["z"] + 2 * d + b
                    act.wait_ge(filled, FULL["z"] + 2 * d + b)
                    for k in range(2):
                        h = 2 * b + k
                        c = C_GB + GLA_HEADS * d + h
                        last = nc.scalar.activation(lt[:, d, h, :], ring[:, g % 4, k * S:(k + 1) * S], ACT.Abs,
                                                    bias=par[:, c:c + 1])
                        own.mark(last) if k == 0 else last.then_inc(z_abs, 1)
                split(6 + d)
            act.wait_ge(z_abs, 4)
            for d in range(2):
                own.wait()
                own.mark(nc.scalar.activation(lt[:, d, :, :], lt[:, d, :, :], ACT.Exp, scale=-1.0))
                own.wait()
                nc.scalar.activation(lt[:, d, :, :], lt[:, d, :, :], ACT.Ln, bias=1.0).then_inc(soft_ready, 1)
                split(8 + d)

            def exps(h):
                act.wait_ge(dd_ready, h + 1)
                if h:
                    act.wait_ge(prod_ready, h)
                nc.scalar.activation(ep[:, :, :], la[:, :, h, :], ACT.Exp, scale=1.0 / GATE_NORM).then_inc(exps_ready, 1)
                nc.scalar.activation(en[:, :, :], la[:, :, h, :], ACT.Exp, scale=-1.0 / GATE_NORM).then_inc(exps_ready, 1)
                nc.scalar.activation(ed[:, :, :], dd[:, :, :], ACT.Exp, scale=1.0 / GATE_NORM).then_inc(exps_ready, 1)

            exps(0)
            act.wait_ge(used, U_V + 4)
            for t in range(T):
                nc.scalar.activation(v[:, t, :], acc[:, t, :], ACT.Copy).then_inc(v_ready, 1)
            split(10)
            exps(1)
            split(11)
            act.wait_ge(used, U_G + 4)
            for t in range(T):
                nc.scalar.activation(sg[:, t, :], acc[:, t, :], ACT.Silu).then_inc(sg_ready, 1)
            split(12)
            split(13)
            exps(2)
            exps(3)
            split(14)
            split(15)
            act.wait_ge(filled, FULL["o"])
            for t in range(T):
                for h in range(GLA_HEADS):
                    c = GLA_HEADS * t + h
                    last = nc.scalar.activation(xn[:, t, h * GLA_DV:(h + 1) * GLA_DV], acc[:, t, h * GLA_DV:(h + 1) * GLA_DV],
                                                ACT.Square, accum_out=stat[:, c:c + 1])
                    own.mark(last) if h < GLA_HEADS - 1 else last.then_inc(sumsq, 1)
            split(16)
            split(17)
            for b in range(4):
                act.wait_ge(filled, FULL["turn"] + b)
                nc.scalar.activation(h_hi[:, 2 * b:2 * b + 2, :], ring[:, (GEN["turn"] + b) % 4, :].rearrange("p (k s) -> p k s", k=2),
                                     ACT.Copy).then_inc(h_hi_ready, 1)

            def ffn(n):
                B, G, C, J = U_FFN[n], GEN[f"ffn{n}"], C_FFN[n], STEP_FFN[n]

                def taps(e, i, k):
                    act.wait_ge(used, up_unit(B, e, k) + 1 + 6 * i)
                    for half in range(2):
                        c = C + 8 * (2 * e + k) + 4 * half + 32 * i
                        last = nc.scalar.activation(cacc[:, k, half, :], ring[:, (G + 2 * e + k) % 4, half * S:(half + 1) * S],
                                                    ACT.Identity, scale=par[:, bass.ds(c + 1, 1)], bias=par[:, bass.ds(c + 3, 1)])
                    last.then_inc(taps_ready, 1)

                def step(e, i=0):
                    taps(e, i, 0)
                    taps(e, i, 1)
                    split(B + 5 + 3 * e, i)
                    act.wait_ge(ring_free, G + 2 * e + 2 + 4 * i)
                    nc.scalar.activation(sgl[:, :, :], cacc[:, :, 1, :], ACT.Silu).then_inc(gate_ready, 1)
                    split(B + 6 + 3 * e, i)
                    act.wait_ge(act_ready, J + e + 1 + 2 * i)
                    act.wait_ge(used, B + 3 * e - 1 + 6 * i)
                    nc.scalar.activation(a_hi[:, e % 2, :, :], actf[:, :, :], ACT.Copy).then_inc(a_hi_ready, 1)
                    split(B + 7 + 3 * e, i)

                step(0)
                with act.Fori(0, FFN_ITERS // 2) as i:
                    for e in (1, 2):
                        step(e, i)

            for u in range(18, 20):
                split(u)
            for t in range(T):
                sums(t, "ffn0")
            split(20)
            turned("ffn0")
            ffn(0)

            for t in range(T):
                sums(t, "mix1")
            turned("mix1")
            split(U_KV + 5)
            act.wait_ge(ring_free, GEN["kv"] + 2)
            nc.scalar.activation(sq[:, 0:T * KV_HEADS * HD].rearrange("p (t n) -> p t n", t=T), kv[:, :, 0:KV_HEADS * HD],
                                 ACT.Square).then_inc(sq_ready, 1)
            split(U_AO)
            split(U_AO + 1)
            for t in range(T):
                act.wait_ge(used, U_AQ + 4)
                act.wait_ge(head_sumsq, t + 1)
                nc.scalar.activation(sq[:, :], acc[:, t, :], ACT.Square).then_inc(sq_ready, 1)
            split(U_AO + 2)
            split(U_AO + 3)
            for h in range(Q_HEADS + 2):
                if h < Q_HEADS:
                    g = GEN["heads"] + HEAD_AT["s", h]
                    act.wait_ge(nb_ready, h + 1)
                    for t in range(T):
                        nc.scalar.activation(pm[:, h % 2, t, :], ring[:, g % 4, t * S:(t + 1) * S], ACT.Exp,
                                             bias=nb[:, h % 2, t:t + 1], scale=HD ** -0.5,
                                             accum_out=sm[:, h % 2, t:t + 1]).then_inc(exp_ready, 1)
                if h >= 2:
                    act.wait_ge(filled, FULL["heads"] + HEAD_AT["o", h - 2])
                    g = GEN["heads"] + HEAD_AT["o", h - 2]
                    nc.scalar.activation(h_hi[:, h - 2, :], ring[:, g % 4, 0:S], ACT.Copy).then_inc(h_hi_ready, 1)
                if h in (2, 5):
                    split(U_AO + 4 + h // 5)
            for u in range(U_AO + 6, U_AO + 8):
                split(u)
            for t in range(T):
                sums(t, "ffn1")
            split(U_FFN[1] + 4)
            turned("ffn1")
            ffn(1)

            for t in range(T):
                sums(t, "lru")
            turned("lru")
            for e in range(LRU_ITERS):
                plan = LRU_AHEAD[e]
                act.wait_ge(used, LRU_UNIT["x", e] + 1)
                for k in range(2):
                    c = C_LCONV + 5 * (2 * e + k)
                    last = nc.scalar.activation(xc[:, k, :], ring[:, BRANCH_BANK, k * S:(k + 1) * S], ACT.Identity,
                                                scale=par[:, c + 3:c + 4], bias=par[:, c + 4:c + 5])
                last.then_inc(taps_ready, 1)
                act.wait_ge(used, LRU_UNIT["g", e] + 1)
                nc.scalar.activation(sgate[:, :, :], ring[:, GATE_BANK, :].rearrange("p (k s) -> p k s", k=2),
                                     ACT.Sigmoid).then_inc(gate_ready, 1)
                for u in plan[:2]:
                    split(u)
                for k in range(2):
                    act.wait_ge(filled, FULL["lru"] + 2 * e + k)
                    for r, buf in ((0, rg), (1, ig)):
                        c = C_LGB + 2 * (2 * e + k) + r
                        last = nc.scalar.activation(buf[:, k, :], ring[:, HEAD_BANK + k, r * S:(r + 1) * S],
                                                    ACT.Sigmoid, bias=par[:, c:c + 1])
                        own.mark(last) if r == 0 else last.then_inc(ri_ready, 1)
                own.wait()
                if e == 0:
                    act.wait_ge(sp4_ready, 1)
                for k in range(2):
                    h = 2 * e + k
                    nc.scalar.activation(ug[:, k, :], rg[:, k, :], ACT.Tanh, scale=sp4[:, h:h + 1]).then_inc(tanh_ready, 1)
                act.wait_ge(tanh_ready, 2 * e + 2)
                for u in plan[2:3]:
                    split(u)
                nc.scalar.activation(su[:, :, :], ug[:, :, :], ACT.Sqrt, scale=4.0).then_inc(sqrt_ready, 1)
                for u in plan[3:]:
                    split(u)
                act.wait_ge(act_ready, STEP_LRU + e + 1)
                act.wait_ge(used, LRU_UNIT["d", e - 2] + 1 if e >= 2 else U_LRU)
                nc.scalar.activation(a_hi[:, e % 2, :, :], actl[:, :, :], ACT.Copy).then_inc(a_hi_ready, 1)

            for t in range(T):
                sums(t, "sc")
            turned("sc")
            split(U_SC + 4, half=True)

            def sc_step(e, i=0, splits=3):
                act.wait_ge(used, up_unit(U_SC, e, 0) + 1 + 6 * i)
                nc.scalar.activation(cgs[:, :], ring[:, (GEN["sc"] + 2 * e) % 4, 0:S], ACT.Copy).then_inc(cg_ready, 1)
                act.wait_ge(used, up_unit(U_SC, e, 1) + 1 + 6 * i)
                nc.scalar.activation(sgs[:, :], ring[:, (GEN["sc"] + 2 * e + 1) % 4, S:2 * S], ACT.Silu).then_inc(gate_ready, 1)
                for k in range(splits):
                    if k == 1:
                        ahead(e, i)
                    split(U_SC + 5 + 3 * e + k, i, half=sc_half(U_SC + 5 + 3 * e + k))
                if splits < 2:
                    ahead(e, i)
                act.wait_ge(act_ready, STEP_SC + e + 1 + 2 * i)
                act.wait_ge(used, U_SC + 3 * e - 1 + 6 * i)
                nc.scalar.activation(a_hi[:, e % 2, 0, :], acts[:, :], ACT.Copy).then_inc(a_hi_ready, 1)

            def ahead(e, i):
                c = C_SCONV + 3 * e + 6 * i
                act.wait_ge(ring_free, GEN["sc"] + 2 * e + 1 + 4 * i)
                nc.scalar.activation(ct[:, :], pp[:, :], ACT.Identity, scale=par[:, bass.ds(c + 2, 1)], bias=0.0).then_inc(taps_ready, 1)

            sc_step(0)
            with act.Fori(0, (SC_ITERS - 4) // 2) as i:
                for e in (1, 2):
                    sc_step(e, i)
            sc_step(SC_ITERS - 3)
            sc_step(SC_ITERS - 2, splits=1)
            sc_step(SC_ITERS - 1, splits=0)
            for t in range(T):
                sums(t, "final")

        @block.vector
        def _(dve):
            own = Chain(dve, dve_own)

            def split(u, i=0, half=False):
                n = UNIT // 2 if half else UNIT
                dve.wait_ge(hi_split, u + 1 + RING * i)
                nc.vector.tensor_tensor(w_lo[:, u % RING, 0:n], raw[:, u % RAW, 0:n], w_hi[:, u % RING, 0:n].bitcast(f32),
                                        ALU.subtract).then_inc(lo_split, 1)

            def normed(name):
                for t in range(T):
                    dve.wait_ge(rms_ready, RMS[name] + t + 1)
                    nc.vector.tensor_scalar(xn[:, t, :], x[:, t, :], rstd[:, t:t + 1], None, ALU.mult).then_inc(xn_ready, 1)

            def turned(name):
                for b in range(4):
                    dve.wait_ge(h_hi_ready, HH[name] + b + 1)
                    for k in range(2):
                        kc = 2 * b + k
                        c = C_GAMMA[name] + kc
                        last = nc.vector.scalar_tensor_tensor(
                            out=h_lo[:, kc, :], in0=ring[:, (GEN["norm_" + name] + b) % 4, k * S:(k + 1) * S],
                            scalar=par[:, c:c + 1], in1=h_hi[:, kc, :].bitcast(f32), op0=ALU.mult, op1=ALU.subtract)
                    last.then_inc(ring_free, 1)

            def residual(units):
                dve.wait_ge(used, units)
                for t in range(T):
                    nc.vector.tensor_tensor(x[:, t, :], acc[:, t, :], x[:, t, :], ALU.add).then_inc(acc_free[t], 1)

            def two(bank):
                return ring[:, bank % 4, :].rearrange("p (k s) -> p k s", k=2)

            dve.wait_ge(x_loaded, 16)
            normed("mix0")
            split(0)
            split(1)
            dve.wait_ge(consts_loaded, 16 * N_CONSTS)
            turned("mix0")
            dve.wait_ge(lam_ready, 1)
            own.mark(nc.vector.tensor_scalar(lam_q[:, :], lam_e[:, :], 2.0, None, ALU.add))
            own.wait()
            own.mark(nc.vector.reciprocal(lam_p[:, :], lam_q[:, :]))
            own.wait()
            own.mark(nc.vector.tensor_tensor(lam_s[:, :], lam_e[:, :], lam_p[:, :], ALU.mult))
            own.wait()
            own.mark(nc.vector.tensor_tensor(lam_q[:, :], lam_s[:, :], lam_s[:, :], ALU.mult))
            own.mark(nc.vector.memset(lam_p[:, :], 1.0 / 17))
            for n in (15, 13, 11, 9, 7, 5, 3, 1):
                own.wait()
                own.mark(nc.vector.tensor_tensor(lam_p[:, :], lam_p[:, :], lam_q[:, :], ALU.mult))
                own.wait()
                own.mark(nc.vector.tensor_scalar(lam_p[:, :], lam_p[:, :], 1.0 / n, None, ALU.add))
            own.wait()
            own.mark(nc.vector.tensor_tensor(lam_p[:, :], lam_p[:, :], lam_s[:, :], ALU.mult))
            own.mark(nc.vector.tensor_scalar(lam_q[:, :], par[:, C_LAM:C_LAM + LRU_HEADS], -1.0, 0.0, ALU.mult, ALU.max))
            own.wait()
            own.mark(nc.vector.scalar_tensor_tensor(out=lam_p[:, :], in0=lam_p[:, :], scalar=2.0, in1=lam_q[:, :],
                                                    op0=ALU.mult, op1=ALU.add))
            own.wait()
            nc.vector.tensor_scalar(sp4[:, :], lam_p[:, :], LRU_C / 2, None, ALU.mult).then_inc(sp4_ready, 1)
            split(2)
            split(3)
            dve.wait_ge(filled, FULL["rank"])
            nc.vector.tensor_copy(rt[:, :, :], ring[0:GLA_RANK, GEN["rank"] % 4, :].rearrange("p (a s) -> p a s", a=2)).then_inc(ring_free, 1)
            for b in range(2):
                dve.wait_ge(used, U_Q + b + 1)
                nc.vector.tensor_scalar(qT[:, 2 * b:2 * b + 2, :], two(GEN["q"] + b), GLA_DK ** -0.5, None,
                                        ALU.mult).then_inc(ring_free, 1)
            split(4)
            for b in range(2):
                dve.wait_ge(used, U_K + b + 1)
                nc.vector.tensor_copy(kT[:, 2 * b:2 * b + 2, :], two(GEN["k"] + b)).then_inc(ring_free, 1)
            split(5)
            for d in range(2):
                for b in range(2):
                    dve.wait_ge(z_abs, 2 * d + b + 1)
                    for k in range(2):
                        h = 2 * b + k
                        c = C_GB + GLA_HEADS * d + h
                        last = nc.vector.tensor_scalar(la[:, d, h, :], ring[:, (GEN["z"] + 2 * d + b) % 4, k * S:(k + 1) * S],
                                                       par[:, c:c + 1], 0.0, ALU.add, ALU.min)
                        own.mark(last) if k == 0 else last.then_inc(ring_free, 1)
                split(6 + d)
            dve.wait_ge(made, 4)
            for d in range(2):
                dve.wait_ge(soft_ready, d + 1)
                own.wait()
                dve.wait_ge(ring_free, GEN["z"] + 4)
                own.mark(nc.vector.tensor_tensor(lt[:, d, :, :], la[:, d, :, :], lt[:, d, :, :], ALU.subtract))
                own.wait()
                for h in range(GLA_HEADS):
                    order = slice(None) if d == 0 else slice(S - 1, None, -1)
                    own.mark(nc.vector.tensor_tensor_scan(out=la[:, d, h, order], data0=chunk_on[:, :], data1=lt[:, d, h, order],
                                                          initial=0.0, op0=ALU.mult, op1=ALU.add))
                split(8 + d)
            own.wait()

            def differences(h):
                for d in range(2):
                    by_chunk = la[:, d, h, :].rearrange("p (c n) -> p c n", n=CHUNK)
                    end = by_chunk[:, :, CHUNK - 1:CHUNK] if d == 0 else by_chunk[:, :, 0:1]
                    last = nc.vector.tensor_tensor(dd[:, d, :].rearrange("p (c n) -> p c n", n=CHUNK),
                                                   end.to_broadcast([P, S // CHUNK, CHUNK]), by_chunk, ALU.subtract)
                    own.mark(last) if d == 0 else last.then_inc(dd_ready, 1)

            def products(h):
                dve.wait_ge(exps_ready, 3 * h + 3)
                for o, e, s in ((qd, ep, qT), (ki, en, kT), (kd, ed, kT)):
                    own.mark(nc.vector.tensor_tensor(o[:, :, :], e[:, :, :], s[:, h:h + 1, :].to_broadcast([P, 2, S]), ALU.mult))
                own.wait()
                C = CHUNK
                own.mark(nc.vector.tensor_scalar(kt[:, 0, 0:C], kd[:, 0, 0:C], ep[:, 0, 2 * C - 1:2 * C], None, ALU.mult))
                own.mark(nc.vector.tensor_copy(kt[:, 0, C:2 * C], kd[:, 0, C:2 * C]))
                own.mark(nc.vector.tensor_copy(qt[:, 0, 0:C], qd[:, 0, 2 * C:3 * C]))
                own.mark(nc.vector.tensor_scalar(qt[:, 0, C:2 * C], qd[:, 0, 3 * C:4 * C], ep[:, 0, 3 * C - 1:3 * C], None, ALU.mult))
                own.mark(nc.vector.tensor_copy(kt[:, 1, 0:C], kd[:, 1, 2 * C:3 * C]))
                own.mark(nc.vector.tensor_scalar(kt[:, 1, C:2 * C], kd[:, 1, 3 * C:4 * C], ep[:, 1, 2 * C:2 * C + 1], None, ALU.mult))
                own.mark(nc.vector.tensor_scalar(qt[:, 1, 0:C], qd[:, 1, 0:C], ep[:, 1, C:C + 1], None, ALU.mult))
                nc.vector.tensor_copy(qt[:, 1, C:2 * C], qd[:, 1, C:2 * C]).then_inc(prod_ready, 1)

            def scores(h):
                g = GEN["att"] + 2 * h
                dve.wait_ge(filled, FULL["att"] + 2 * h)
                if h == 0:
                    dve.wait_ge(sg_ready, T)
                own.mark(nc.vector.tensor_copy(att_c[:, h % 2, :, :], ring[:, g % 4, T * P:2 * T * P].rearrange("p (t c) -> p t c", t=T)))
                own.wait()
                nc.vector.copy_predicated(att_c[:, h % 2, :, :], causal[:, :, :].bitcast(u32),
                                          ring[:, g % 4, 0:T * P].rearrange("p (t c) -> p t c", t=T)).then_inc(ring_free, 1)
                dve.wait_ge(filled, FULL["att"] + 2 * h + 1)
                nc.vector.tensor_copy(att_x[:, h % 2, :, :], ring[:, (g + 1) % 4, 0:T * P].rearrange("p (t c) -> p t c", t=T)).then_inc(ring_free, 1)

            differences(0)
            products(0)
            differences(1)
            split(10)
            split(11)
            for t in range(T):
                dve.wait_ge(sg_ready, t + 1)
                by_head = sg[:, t, :].rearrange("p (h n) -> p h n", h=GLA_HEADS)
                own.mark(nc.vector.tensor_tensor(by_head, by_head, row[:, R_GLA:R_GLA + GLA_DV].unsqueeze(1).to_broadcast(
                    [P, GLA_HEADS, GLA_DV]), ALU.mult))
            split(12)
            split(13)
            scores(0)
            for h in range(1, GLA_HEADS):
                products(h)
                if h + 1 < GLA_HEADS:
                    differences(h + 1)
                scores(h)
            split(14)
            split(15)
            own.wait()
            for t in range(T):
                dve.wait_ge(rms_ready, RMS["gla"] + t + 1)
                for h in range(GLA_HEADS):
                    at = slice(h * GLA_DV, (h + 1) * GLA_DV)
                    c = GLA_HEADS * t + h
                    last = nc.vector.scalar_tensor_tensor(out=xn[:, t, at], in0=acc[:, t, at], scalar=rstd[:, c:c + 1],
                                                          in1=sg[:, t, at], op0=ALU.mult, op1=ALU.mult)
                    own.mark(last) if h < GLA_HEADS - 1 else last.then_inc(xn_ready, 1)
            split(16)
            split(17)
            for b in range(4):
                dve.wait_ge(h_hi_ready, HH["turn"] + b + 1)
                nc.vector.tensor_tensor(h_lo[:, 2 * b:2 * b + 2, :], two(GEN["turn"] + b), h_hi[:, 2 * b:2 * b + 2, :].bitcast(f32),
                                        ALU.subtract).then_inc(ring_free, 1)
            split(18)
            split(19)
            residual(U_GO + 4)

            def ffn(n):
                B, G, C, J = U_FFN[n], GEN[f"ffn{n}"], C_FFN[n], STEP_FFN[n]

                def conv(e, i, k):
                    dve.wait_ge(taps_ready, 2 * J + 2 * e + k + 1 + 4 * i)
                    bank = (G + 2 * e + k) % 4
                    for tap, out_at, in_at in ((0, slice(1, S), slice(0, S - 1)), (2, slice(0, S - 1), slice(1, S))):
                        for half in range(2):
                            c = C + 8 * (2 * e + k) + 4 * half + tap + 32 * i
                            lo = half * S
                            last = nc.vector.scalar_tensor_tensor(
                                out=cacc[:, k, half, out_at], in0=ring[:, bank, lo + in_at.start:lo + in_at.stop],
                                scalar=par[:, bass.ds(c, 1)], in1=cacc[:, k, half, out_at], op0=ALU.mult, op1=ALU.add)
                            if (tap, half) != (2, 1):
                                own.mark(last)
                        if tap == 0:
                            own.wait()
                    last.then_inc(ring_free, 1)

                def step(e, i=0):
                    conv(e, i, 0)
                    conv(e, i, 1)
                    split(B + 5 + 3 * e, i)
                    dve.wait_ge(gate_ready, J + e + 1 + 2 * i)
                    own.wait()
                    nc.vector.tensor_tensor(actf[:, :, :], cacc[:, :, 0, :], sgl[:, :, :], ALU.mult).then_inc(act_ready, 1)
                    split(B + 6 + 3 * e, i)
                    dve.wait_ge(a_hi_ready, J + e + 1 + 2 * i)
                    nc.vector.tensor_tensor(a_lo[:, e % 2, :, :], actf[:, :, :], a_hi[:, e % 2, :, :].bitcast(f32),
                                            ALU.subtract).then_inc(a_lo_ready, 1)
                    split(B + 7 + 3 * e, i)

                step(0)
                with dve.Fori(0, FFN_ITERS // 2) as i:
                    own.enter(12, i)
                    for e in (1, 2):
                        step(e, i)
                own.leave(FFN_ITERS // 2)

            normed("ffn0")
            split(20)
            turned("ffn0")
            ffn(0)
            residual(U_FFN[0] + FFN_UNITS)

            normed("mix1")
            turned("mix1")
            split(U_KV + 5)
            dve.wait_ge(used, U_KV + 2)
            for t in range(T):
                nc.vector.tensor_copy(kv[:, t, :], ring[:, (GEN["kv"] + t) % 4, :]).then_inc(ring_free, 1)
            split(U_AO)

            def rotate(o, a, tmp, heads, n, t):
                half = HD // 2
                view = a.rearrange("p (h a n) -> p h a n", h=heads, a=2)
                own.mark(nc.vector.tensor_tensor(o.rearrange("p (h n) -> p h n", h=heads), a.rearrange("p (h n) -> p h n", h=heads),
                                                 tabs[:, n, 0, t, :].unsqueeze(1).to_broadcast([P, heads, HD]), ALU.mult))
                for side in range(2):
                    own.mark(nc.vector.tensor_tensor(
                        tmp.rearrange("p (h a n) -> p h a n", h=heads, a=2)[:, :, side, :], view[:, :, 1 - side, :],
                        tabs[:, n, 1, t, side * half:(side + 1) * half].unsqueeze(1).to_broadcast([P, heads, half]), ALU.mult))
                own.wait()
                return nc.vector.tensor_tensor(o, o, tmp, ALU.add)

            NK = T * KV_HEADS
            dve.wait_ge(sq_ready, 1)
            nc.vector.tensor_reduce(out=stat[:, 16:16 + NK], in_=sq[:, 0:NK * HD].rearrange("p (g n) -> p g n", g=NK),
                                    axis=AX.X, op=ALU.add).then_inc(head_sumsq, 1)
            split(U_AO + 1)
            dve.wait_ge(rms_ready, RMS["k"] + 1)
            dve.wait_ge(tables_ready, 6)
            for t in range(T):
                scale = rstd[:, 16 + t * KV_HEADS:16 + (t + 1) * KV_HEADS].unsqueeze(2).to_broadcast([P, KV_HEADS, HD])
                own.mark(nc.vector.tensor_tensor(kn[:, t, :].rearrange("p (h n) -> p h n", h=KV_HEADS),
                                                 kv[:, t, 0:KV_HEADS * HD].rearrange("p (h n) -> p h n", h=KV_HEADS), scale, ALU.mult))
                own.wait()
                rotate(kr[:, t, :], kn[:, t, :], rtmp[:, t * 256:t * 256 + KV_HEADS * HD], KV_HEADS, 1, t).then_inc(roped, 1)
            dve.wait_ge(roped, T)
            for t in range(T):
                dve.wait_ge(sq_ready, t + 2)
                nc.vector.tensor_reduce(out=stat[:, t * Q_HEADS:(t + 1) * Q_HEADS],
                                        in_=sq[:, :].rearrange("p (g n) -> p g n", g=Q_HEADS), axis=AX.X, op=ALU.add).then_inc(head_sumsq, 1)
                dve.wait_ge(rms_ready, RMS["q"] + t + 1)
                scale = rstd[:, t * Q_HEADS:(t + 1) * Q_HEADS].unsqueeze(2).to_broadcast([P, Q_HEADS, HD])
                nc.vector.tensor_tensor(qn[:, t, :].rearrange("p (h n) -> p h n", h=Q_HEADS),
                                        acc[:, t, :].rearrange("p (h n) -> p h n", h=Q_HEADS), scale, ALU.mult).then_inc(acc_free[t], 1)
                dve.wait_ge(acc_free[t], FREED["ao"])
                rotate(qr[:, t, :], qn[:, t, :], rtmp[:, :], Q_HEADS, 0, t).then_inc(roped, 1)
                dve.wait_ge(roped, T + t + 1)
            dve.wait_ge(filled, FULL["kT"])
            nc.vector.tensor_copy(kT2[:, :, :], two(GEN["kT"])).then_inc(ring_free, 1)
            for b in range(4):
                dve.wait_ge(filled, FULL["qT"] + b)
                nc.vector.tensor_copy(qT2[:, 2 * b:2 * b + 2, :], two(GEN["qT"] + b)).then_inc(ring_free, 1)
            split(U_AO + 2)
            split(U_AO + 3)
            for h in range(Q_HEADS + 2):
                if h < Q_HEADS:
                    at = HEAD_AT["s", h]
                    dve.wait_ge(filled, FULL["heads"] + at)
                    own.mark(nc.vector.reduce_max(mx[:, h % 2, :], two(GEN["heads"] + at), AX.X))
                    own.wait()
                    nc.vector.tensor_scalar(nb[:, h % 2, :], mx[:, h % 2, :], -HD ** -0.5, None, ALU.mult).then_inc(nb_ready, 1)
                    dve.wait_ge(exp_ready, 2 * h + 2)
                    own.mark(nc.vector.reciprocal(mx[:, h % 2, :], sm[:, h % 2, :]))
                    own.wait()
                    nc.vector.tensor_tensor(pm[:, h % 2, :, :], pm[:, h % 2, :, :], mx[:, h % 2, :].unsqueeze(2).to_broadcast([P, T, S]),
                                            ALU.mult).then_inc(ring_free, 1)
                if 1 <= h <= Q_HEADS:
                    at = HEAD_AT["p", h - 1]
                    dve.wait_ge(filled, FULL["heads"] + at)
                    nc.vector.tensor_copy(pt[:, (h - 1) % 2, :, :], two(GEN["heads"] + at)).then_inc(ring_free, 1)
                if h >= 2:
                    at = HEAD_AT["o", h - 2]
                    dve.wait_ge(h_hi_ready, HH["heads"] + h - 1)
                    nc.vector.tensor_tensor(h_lo[:, h - 2, :], ring[:, (GEN["heads"] + at) % 4, 0:S], h_hi[:, h - 2, :].bitcast(f32),
                                            ALU.subtract).then_inc(ring_free, 1)
                if h in (2, 5):
                    split(U_AO + 4 + h // 5)
            for u in range(U_AO + 6, U_AO + 8):
                split(u)
            residual(U_AO + 4)
            normed("ffn1")
            split(U_FFN[1] + 4)
            turned("ffn1")
            ffn(1)
            residual(U_FFN[1] + FFN_UNITS)

            normed("lru")
            turned("lru")
            for e in range(LRU_ITERS):
                plan = LRU_AHEAD[e]
                dve.wait_ge(taps_ready, 2 * STEP_LRU + e + 1)
                bank = BRANCH_BANK
                for back in (1, 2, 3):
                    for k in range(2):
                        c = C_LCONV + 5 * (2 * e + k) + 3 - back
                        last = nc.vector.scalar_tensor_tensor(
                            out=xc[:, k, back:S], in0=ring[:, bank, k * S:(k + 1) * S - back], scalar=par[:, c:c + 1],
                            in1=xc[:, k, back:S], op0=ALU.mult, op1=ALU.add)
                        if (back, k) != (3, 1):
                            own.mark(last)
                    if back < 3:
                        own.wait()
                last.then_inc(branch_free, 1)
                dve.wait_ge(gate_ready, STEP_LRU + e + 1)
                nc.vector.tensor_tensor(gg[:, :, :], two(GATE_BANK), sgate[:, :, :], ALU.mult).then_inc(gate_free, 1)
                for u in plan[:2]:
                    split(u)
                own.wait()
                dve.wait_ge(branch_free, e + 1)
                dve.wait_ge(ri_ready, 2 * e + 2)
                nc.vector.tensor_tensor(iu[:, :, :], ig[:, :, :], xc[:, :, :], ALU.mult).then_inc(heads_free, 1)
                dve.wait_ge(tanh_ready, 2 * e + 2)
                own.mark(nc.vector.tensor_scalar(p1[:, :, :], ug[:, :, :], 1.0, None, ALU.add))
                own.wait()
                own.mark(nc.vector.reciprocal(rr[:, :, :], p1[:, :, :]))
                own.wait()
                own.mark(nc.vector.scalar_tensor_tensor(out=aa[:, :, :], in0=ug[:, :, :], scalar=1.0, in1=rr[:, :, :],
                                                        op0=ALU.subtract, op1=ALU.mult, reverse0=True))
                dve.wait_ge(sqrt_ready, e + 1)
                own.mark(nc.vector.tensor_tensor(p1[:, :, :], su[:, :, :], rr[:, :, :], ALU.mult))
                own.wait()
                dve.wait_ge(heads_free, e + 1)
                own.mark(nc.vector.tensor_tensor(iu[:, :, :], p1[:, :, :], iu[:, :, :], ALU.mult))
                own.wait()
                for k in range(2):
                    own.mark(nc.vector.tensor_tensor_scan(out=yy[:, k, :], data0=aa[:, k, :], data1=iu[:, k, :], initial=0.0,
                                                          op0=ALU.mult, op1=ALU.add))
                own.wait()
                dve.wait_ge(gate_free, e + 1)
                nc.vector.tensor_tensor(actl[:, :, :], yy[:, :, :], gg[:, :, :], ALU.mult).then_inc(act_ready, 1)
                for u in plan[2:]:
                    split(u)
                dve.wait_ge(a_hi_ready, STEP_LRU + e + 1)
                nc.vector.tensor_tensor(a_lo[:, e % 2, :, :], actl[:, :, :], a_hi[:, e % 2, :, :].bitcast(f32),
                                        ALU.subtract).then_inc(a_lo_ready, 1)
            residual(U_SC)

            normed("sc")
            turned("sc")
            split(U_SC + 4, half=True)

            def sc_step(e, i=0, splits=3):
                g = GEN["sc"] + 2 * e
                dve.wait_ge(cg_ready, e + 1 + 2 * i)
                nc.vector.tensor_tensor(pp[:, :], ring[:, g % 4, S:2 * S], cgs[:, :], ALU.mult).then_inc(ring_free, 1)
                for k in range(splits):
                    if k == 1:
                        taps(e, i)
                    split(U_SC + 5 + 3 * e + k, i, half=sc_half(U_SC + 5 + 3 * e + k))
                if splits < 2:
                    taps(e, i)
                dve.wait_ge(a_hi_ready, STEP_SC + e + 1 + 2 * i)
                nc.vector.tensor_tensor(a_lo[:, e % 2, 0, :], acts[:, :], a_hi[:, e % 2, 0, :].bitcast(f32),
                                        ALU.subtract).then_inc(a_lo_ready, 1)

            def taps(e, i):
                g = GEN["sc"] + 2 * e
                c = C_SCONV + 3 * e + 6 * i
                dve.wait_ge(taps_ready, 2 * STEP_LRU + LRU_ITERS + e + 1 + 2 * i)
                own.mark(nc.vector.scalar_tensor_tensor(out=ct[:, 1:S], in0=pp[:, 0:S - 1], scalar=par[:, bass.ds(c + 1, 1)],
                                                        in1=ct[:, 1:S], op0=ALU.mult, op1=ALU.add))
                own.wait()
                own.mark(nc.vector.scalar_tensor_tensor(out=ct[:, 2:S], in0=pp[:, 0:S - 2], scalar=par[:, bass.ds(c, 1)],
                                                        in1=ct[:, 2:S], op0=ALU.mult, op1=ALU.add))
                own.wait()
                dve.wait_ge(gate_ready, STEP_SC + e + 1 + 2 * i)
                nc.vector.tensor_tensor(ys[:, :], ring[:, (g + 1) % 4, 0:S], ct[:, :], ALU.mult).then_inc(ring_free, 1)
                dve.wait_ge(ring_free, g + 2 + 4 * i)
                nc.vector.tensor_tensor(acts[:, :], ys[:, :], sgs[:, :], ALU.mult).then_inc(act_ready, 1)

            sc_step(0)
            with dve.Fori(0, (SC_ITERS - 4) // 2) as i:
                own.enter(4, i)
                for e in (1, 2):
                    sc_step(e, i)
            own.leave((SC_ITERS - 4) // 2)
            sc_step(SC_ITERS - 3)
            sc_step(SC_ITERS - 2, splits=1)
            sc_step(SC_ITERS - 1, splits=0)
            residual(UNITS)
            for t in range(T):
                dve.wait_ge(rms_ready, RMS["final"] + t + 1)
                nc.vector.scalar_tensor_tensor(out=xn[:, t, :], in0=x[:, t, :], scalar=rstd[:, t:t + 1],
                                               in1=row[:, R_FINAL:R_FINAL + D], op0=ALU.mult, op1=ALU.mult).then_inc(out_ready, 1)

        @block.tensor
        def _(pe):
            PARTS = ((0, 0), (0, 1), (1, 0))
            h_parts, w_parts, a_parts = (h_hi, h_lo), (w_hi, w_lo), (a_hi, a_lo)

            def ready(u, i=0):
                pe.wait_ge(lo_split, u + 1 + RING * i)

            def bank(g, i=0):
                if g >= 4:
                    pe.wait_ge(ring_free, g - 3 + 4 * i)

            def turn(name, g0, f_hook=None):
                for t in range(T):
                    pe.wait_ge(xn_ready, XN[name] + t + 1)
                    for kc in range(KC):
                        g = g0 + kc // 2
                        if t == 0 and kc % 2 == 0:
                            bank(g)
                        lo = (kc % 2) * S + t * P
                        last = nc.tensor.transpose(ring[:, g % 4, lo:lo + P], xn[:, t, kc * P:(kc + 1) * P], ident[:, :])
                        if t == T - 1 and kc % 2 == 1:
                            last.then_inc(filled, 1)

            def wide(u, b, i=0, h_count=None, g=None, free=None):
                ready(u, i)
                if free is not None:
                    pe.wait_ge(*free)
                if g is not None:
                    bank(g, i)
                slot = u % RING
                for f in range(2):
                    for kc in range(KC):
                        if h_count is not None and f == 0 and kc % 2 == 0:
                            pe.wait_ge(ring_free, h_count + kc // 2 + 1)
                        for n, (a, c) in enumerate(PARTS):
                            lo = kc * 256 + f * P
                            last = nc.tensor.matmul(ring[:, b, f * S:(f + 1) * S], w_parts[a][:, slot, lo:lo + P],
                                                    h_parts[c][:, kc, :], start=kc == 0 and n == 0,
                                                    stop=kc == KC - 1 and n == 2, skip_group_check=True)
                last.then_inc(used, 1)

            def tall(u, lhs, kcs, first, end, i=0):
                ready(u, i)
                slot = u % RING
                for j, kc in enumerate(kcs):
                    for t in range(T):
                        for half in range(2):
                            for n, (a, c) in enumerate(PARTS):
                                last = nc.tensor.matmul(acc[:, t, half * 512:(half + 1) * 512], lhs(a, kc, t),
                                                        w_parts[c][:, slot, j * D + half * 512:j * D + (half + 1) * 512],
                                                        start=first and j == 0 and n == 0,
                                                        stop=end and j == len(kcs) - 1 and n == 2, skip_group_check=True)
                last.then_inc(used, 1)

            def of_h(a, kc, t):
                return h_parts[a][:, kc, t * P:(t + 1) * P]

            def project(u0):
                for n in range(4):
                    tall(u0 + n, of_h, (2 * n, 2 * n + 1), first=n == 0, end=n == 3)

            def clear_acc():
                for t in range(T):
                    for half in range(2):
                        nc.tensor.matmul(acc[:, t, half * 512:(half + 1) * 512], zeros[:, 0:P], zeros[:, :],
                                         start=True, stop=False, skip_group_check=True)

            pe.wait_ge(made, 4)
            turn("mix0", GEN["norm_mix0"])
            pe.wait_ge(consts_loaded, 16 * N_CONSTS)
            g = GEN["rank"]
            bank(g)
            for kc in range(KC):
                if kc % 2 == 0:
                    pe.wait_ge(ring_free, GEN["norm_mix0"] + kc // 2 + 1)
            for d in range(2):
                for kc in range(KC):
                    n = 0
                    for part in h_parts:
                        last = nc.tensor.matmul(ring[0:GLA_RANK, g % 4, d * S:(d + 1) * S],
                                                wr[:, kc, d * GLA_RANK:(d + 1) * GLA_RANK], part[:, kc, :].bitcast(f32),
                                                start=kc == 0 and n == 0, stop=kc == KC - 1 and n == 1, skip_group_check=True)
                        n += 1
            last.then_inc(filled, 1)
            for u, g in ((U_Q, GEN["q"]), (U_Q + 1, GEN["q"] + 1), (U_K, GEN["k"]), (U_K + 1, GEN["k"] + 1)):
                wide(u, g % 4, g=g)
            for d in range(2):
                for b in range(2):
                    g = GEN["z"] + 2 * d + b
                    bank(g)
                    for k in range(2):
                        h = 2 * b + k
                        last = nc.tensor.matmul(ring[:, g % 4, k * S:(k + 1) * S], gup[:, d, h * P:(h + 1) * P], rt[:, d, :],
                                                start=True, stop=True, skip_group_check=True)
                    last.then_inc(filled, 1)
            project(U_V)
            pe.wait_ge(v_ready, T)
            project(U_G)

            def scores(h):
                pe.wait_ge(prod_ready, h + 1)
                g = GEN["att"] + 2 * h
                bank(g)
                C = CHUNK
                for t in range(T):
                    lo = t * P
                    nc.tensor.matmul(ring[:, g % 4, lo:lo + P], ki[:, 0, lo:lo + P], qd[:, 0, lo:lo + P],
                                     start=True, stop=True, skip_group_check=True)
                    nc.tensor.matmul(ring[0:C, g % 4, lo + C:lo + P], kd[:, 0, lo:lo + C], qd[:, 0, lo + C:lo + P],
                                     start=True, stop=True, skip_group_check=True)
                    up = T * P + lo
                    nc.tensor.matmul(ring[:, g % 4, up:up + P], ki[:, 1, lo:lo + P], qd[:, 1, lo:lo + P],
                                     start=True, stop=True, skip_group_check=True)
                    last = nc.tensor.matmul(ring[C:P, g % 4, up:up + C], kd[:, 1, lo + C:lo + P], qd[:, 1, lo:lo + C],
                                            start=True, stop=True, skip_group_check=True)
                last.then_inc(filled, 1)
                bank(g + 1)
                for d in range(2):
                    last = nc.tensor.matmul(ring[:, (g + 1) % 4, d * P:(d + 1) * P], kt[:, d, :], qt[:, d, :],
                                            start=True, stop=True, skip_group_check=True)
                last.then_inc(filled, 1)

            def outputs(h):
                if h == 0:
                    pe.wait_ge(sg_ready, T)
                pe.wait_ge(ring_free, GEN["att"] + 2 * h + 2)
                for t in range(T):
                    at = slice(h * GLA_DV, (h + 1) * GLA_DV)
                    nc.tensor.matmul(acc[:, t, at], att_c[:, h % 2, t, :], v[:, t, at], start=True, stop=False, skip_group_check=True)
                    last = nc.tensor.matmul(acc[:, t, at], att_x[:, h % 2, 1 - t, :], v[:, 1 - t, at],
                                            start=False, stop=True, skip_group_check=True)
                if h == GLA_HEADS - 1:
                    last.then_inc(filled, 1)

            scores(0)
            for h in range(1, GLA_HEADS):
                scores(h)
                outputs(h - 1)
            outputs(GLA_HEADS - 1)
            turn("gla", GEN["turn"])
            for n in range(4):
                pe.wait_ge(ring_free, GEN["turn"] + n + 1)
                tall(U_GO + n, of_h, (2 * n, 2 * n + 1), first=n == 0, end=n == 3)

            def ffn(n):
                B, G, J = U_FFN[n], GEN[f"ffn{n}"], STEP_FFN[n]

                def up(e, i=0):
                    for k in range(2):
                        g = G + 2 * e + k
                        wide(up_unit(B, e, k), g % 4, i, g=g, h_count=GEN[f"norm_ffn{n}"] if e == 0 else None)

                def down(e, u, i=0, end=False):
                    pe.wait_ge(a_lo_ready, J + e + 1 + 2 * i)
                    tall(u, lambda a, kc, t: a_parts[a][:, e % 2, kc, t * P:(t + 1) * P], (0, 1), False, end, i)

                up(0)
                pe.wait_ge(acc_free[0], FREED[f"ffn{n}"])
                pe.wait_ge(acc_free[1], FREED[f"ffn{n}"])
                clear_acc()
                with pe.Fori(0, FFN_ITERS // 2) as i:
                    for e in (1, 2):
                        up(e, i)
                        down(e - 1, B + 3 * e + 1, i)
                down(FFN_ITERS - 1, B + FFN_UNITS - 1, end=True)

            turn("ffn0", GEN["norm_ffn0"])
            ffn(0)

            turn("mix1", GEN["norm_mix1"])
            for n in range(2):
                ready(U_KV + n)
                for j in range(4):
                    kc = 4 * n + j
                    if kc % 2 == 0:
                        pe.wait_ge(ring_free, GEN["norm_mix1"] + kc // 2 + 1)
                    for t in range(T):
                        g = GEN["kv"] + t
                        if kc == 0:
                            bank(g)
                        for m, (a, c) in enumerate(PARTS):
                            last = nc.tensor.matmul(ring[:, g % 4, :], of_h(a, kc, t), w_parts[c][:, (U_KV + n) % RING, j * 512:(j + 1) * 512],
                                                    start=kc == 0 and m == 0, stop=kc == KC - 1 and m == 2, skip_group_check=True)
                last.then_inc(used, 1)
            project(U_AQ)

            def turn_heads(rows, heads, g0):
                for h in range(heads):
                    g = g0 + h // 2
                    if h % 2 == 0:
                        bank(g)
                    for t in range(T):
                        lo = (h % 2) * S + t * P
                        last = nc.tensor.transpose(ring[:, g % 4, lo:lo + P], rows[:, t, h * HD:(h + 1) * HD], ident[:, :])
                    if h % 2 == 1:
                        last.then_inc(filled, 1)

            pe.wait_ge(roped, T)
            turn_heads(kr, KV_HEADS, GEN["kT"])
            pe.wait_ge(roped, 2 * T)
            turn_heads(qr, Q_HEADS, GEN["qT"])
            for h in range(Q_HEADS + 2):
                if h < Q_HEADS:
                    g = GEN["heads"] + HEAD_AT["s", h]
                    bank(g)
                    if h % 2 == 0:
                        pe.wait_ge(ring_free, GEN["qT"] + h // 2 + 1)
                    for t in range(T):
                        last = nc.tensor.matmul(ring[:, g % 4, t * S:(t + 1) * S], qT2[:, h, t * P:(t + 1) * P], kT2[:, h // GROUP, :],
                                                start=True, stop=True, skip_group_check=True)
                    last.then_inc(filled, 1)
                if 1 <= h <= Q_HEADS:
                    g = GEN["heads"] + HEAD_AT["p", h - 1]
                    bank(g)
                    pe.wait_ge(ring_free, GEN["heads"] + HEAD_AT["s", h - 1] + 1)
                    for t in range(T):
                        for kc in range(T):
                            lo = kc * S + t * P
                            last = nc.tensor.transpose(ring[:, g % 4, lo:lo + P], pm[:, (h - 1) % 2, t, kc * P:(kc + 1) * P], ident[:, :])
                    last.then_inc(filled, 1)
                if h >= 2:
                    g = GEN["heads"] + HEAD_AT["o", h - 2]
                    bank(g)
                    pe.wait_ge(ring_free, GEN["heads"] + HEAD_AT["p", h - 2] + 1)
                    first_v = KV_HEADS * HD + (h - 2) // GROUP * HD
                    for kc in range(T):
                        last = nc.tensor.matmul(ring[:, g % 4, 0:S], kv[:, kc, first_v:first_v + HD], pt[:, h % 2, kc, :],
                                                start=kc == 0, stop=kc == T - 1, skip_group_check=True)
                    last.then_inc(filled, 1)
            for t in range(T):
                pe.wait_ge(acc_free[t], FREED["ao"])
            for n in range(4):
                pe.wait_ge(ring_free, GEN["heads"] + HEAD_AT["o", 2 * n + 1] + 1)
                tall(U_AO + n, of_h, (2 * n, 2 * n + 1), first=n == 0, end=n == 3)
            turn("ffn1", GEN["norm_ffn1"])
            ffn(1)

            turn("lru", GEN["norm_lru"])
            pe.wait_ge(gatew_loaded, 16)
            for j in range(LRU_ITERS + 2):
                if j < LRU_ITERS:
                    first = GEN["norm_lru"] if j == 0 else None
                    wide(LRU_UNIT["x", j], BRANCH_BANK, h_count=first, free=(branch_free, j) if j else (ring_free, GEN["lru"]))
                    wide(LRU_UNIT["g", j], GATE_BANK, free=(gate_free, j) if j else None)
                if 1 <= j <= LRU_ITERS:
                    e = j - 1
                    pe.wait_ge(branch_free, e + 1)
                    if e:
                        pe.wait_ge(heads_free, e)
                    for k in range(2):
                        for r in range(2):
                            last = nc.tensor.matmul(ring[:, HEAD_BANK + k, r * S:(r + 1) * S],
                                                    gatew[:, 2 * e + k, r * P:(r + 1) * P], xc[:, k, :],
                                                    start=True, stop=True, skip_group_check=True)
                        last.then_inc(filled, 1)
                if j >= 2:
                    e = j - 2
                    pe.wait_ge(a_lo_ready, STEP_LRU + e + 1)
                    if e == 0:
                        for t in range(T):
                            pe.wait_ge(acc_free[t], FREED["lru"])
                    tall(LRU_UNIT["d", e], lambda a, kc, t: a_parts[a][:, e % 2, kc, t * P:(t + 1) * P], (0, 1),
                         first=e == 0, end=e == LRU_ITERS - 1)

            turn("sc", GEN["norm_sc"])

            def sc_up(e, i=0):
                for k in range(2):
                    g = GEN["sc"] + 2 * e + k
                    wide(up_unit(U_SC, e, k), g % 4, i, g=g, h_count=GEN["norm_sc"] if e == 0 else None)

            def sc_down(e, u, i=0, end=False):
                pe.wait_ge(a_lo_ready, STEP_SC + e + 1 + 2 * i)
                tall(u, lambda a, kc, t: a_parts[a][:, e % 2, 0, t * P:(t + 1) * P], (0,), False, end, i)

            sc_up(0)
            for t in range(T):
                pe.wait_ge(acc_free[t], FREED["sc"])
            clear_acc()
            with pe.Fori(0, (SC_ITERS - 2) // 2) as i:
                for e in (1, 2):
                    sc_up(e, i)
                    sc_down(e - 1, U_SC + 3 * e + 1, i)
            sc_up(SC_ITERS - 1)
            sc_down(SC_ITERS - 2, U_SC + 3 * (SC_ITERS - 1) + 1)
            sc_down(SC_ITERS - 1, UNITS - 1, end=True)


def wide_unit(w, columns):
    return w[:, columns].reshape(KC, P, 256).transpose(1, 0, 2).reshape(P, UNIT)


def tall_units(w, rows):
    made = w.reshape(-1, rows // P, P, w.shape[1]).transpose(0, 2, 1, 3).reshape(-1, P, rows // P * w.shape[1])
    return list(np.pad(made, ((0, 0), (0, 0), (0, UNIT - made.shape[2]))))


def tiles(a, n=P):
    return np.asarray(a).reshape(-1, n).T


def weight_stream(w):
    tile = lambda first, m: list(range(first + m * P, first + (m + 1) * P))
    units = []
    gla = w["gla_w_in"][0]
    for first in (0, GLA_KEYS):
        for n in range(2):
            units.append(wide_unit(gla, list(range(first + 256 * n, first + 256 * (n + 1)))))
    for first in (2 * GLA_KEYS, 2 * GLA_KEYS + D):
        units += tall_units(gla[:, first:first + D], 256)
    units += tall_units(w["gla_w_out"][0], 256)

    def ffn(n):
        up, down = w["ffn_w_up"][n], tall_units(w["ffn_w_down"][n], 256)
        for e in range(FFN_ITERS):
            for k in range(2):
                units.append(wide_unit(up, tile(0, 2 * e + k) + tile(D_FF, 2 * e + k)))
            if e:
                units.append(down[e - 1])
        units.append(down[-1])

    ffn(0)
    qkv = w["attn_w_qkv"][0]
    units.extend(tall_units(qkv[:, D:], 512))
    units.extend(tall_units(qkv[:, :D], 256))
    units.extend(tall_units(w["attn_w_out"][0], 256))
    ffn(1)
    lru_in, lru_down = w["a_w_in_2"][0], tall_units(w["a_w_out_2"][0], 256)
    lru = {}
    for e in range(LRU_ITERS):
        lru[LRU_UNIT["g", e]] = wide_unit(lru_in, list(range(256 * e, 256 * (e + 1))))
        lru[LRU_UNIT["x", e]] = wide_unit(lru_in, list(range(WIDTH + 256 * e, WIDTH + 256 * (e + 1))))
        lru[LRU_UNIT["d", e]] = lru_down[e]
    units += [lru[u] for u in range(U_LRU, U_SC)]
    sc_in, sc_down = w["b_w_in_2"][0], tall_units(w["b_w_out_2"][0], P)
    for e in range(SC_ITERS):
        units.append(wide_unit(sc_in, tile(WIDTH, e) + tile(2 * WIDTH, e)))
        units.append(wide_unit(sc_in, tile(0, e) + tile(3 * WIDTH, e)))
        if e:
            units.append(sc_down[e - 1])
    units.append(sc_down[-1])
    assert len(units) == UNITS
    return np.stack(units)


def channel_parameters(w):
    cols = [tiles(w["norm_mix"][0]), tiles(w["norm_ffn"][0]), tiles(w["norm_mix"][1]), tiles(w["norm_ffn"][1]),
            tiles(w["norm_g_2"][0]), tiles(w["norm_g_2"][1])]
    for n in range(2):
        taps = np.concatenate([w["ffn_w_conv"][n], w["ffn_b_conv"][n][None]])
        taps = taps.reshape(4, 2, D_FF // P, P).transpose(3, 2, 1, 0)
        cols.append(taps.reshape(P, -1))
    cols += [tiles(w["gla_b_gate_f"][0]), tiles(w["gla_b_gate_b"][0])]
    taps = np.concatenate([w["a_conv_w_2"][0], w["a_conv_b_2"][0][None]])
    cols.append(taps.reshape(5, LRU_HEADS, P).transpose(2, 1, 0).reshape(P, -1))
    cols.append(tiles(w["a_gate_b_2"][0]))
    cols.append(tiles(w["a_lambda_2"][0]))
    cols.append(w["b_conv_w_2"][0].reshape(3, SC_ITERS, P).transpose(2, 1, 0).reshape(P, -1))
    return np.ascontiguousarray(np.concatenate(cols, axis=1))


def rotation():
    grid, pairs = 64, HD // 4
    t = np.arange(S)
    inv = np.float32(10000.0) ** (-np.arange(pairs, dtype=np.float32) / np.float32(pairs))
    ang = np.concatenate([(t // grid).astype(np.float32)[:, None] * inv, (t % grid).astype(np.float32)[:, None] * inv], axis=1)
    cos, sin = np.cos(ang), np.sin(ang)
    both = np.stack([np.concatenate([cos, cos], axis=1), np.concatenate([-sin, sin], axis=1)], axis=1)
    return np.ascontiguousarray(both.reshape(T, P, 2, HD).transpose(1, 0, 2, 3).reshape(P, -1).astype(np.float32))


def kernel(**inputs):
    import concourse.bacc as bacc
    from concourse.bass_utils import run_bass_kernel_spmd

    w = {name: np.asarray(a) for name, a in inputs.items()}
    rank = w["gla_w_in"][0][:, 2 * GLA_KEYS + 2 * D:]
    gate = w["a_gate_w_2"][0].transpose(1, 0, 2).reshape(P, -1)
    arrays = {
        "x": w["x"],
        "stream": weight_stream(w),
        "par": channel_parameters(w),
        "row": np.concatenate([w["final_g_2"], w["gla_norm"][0], w["attn_q_norm"][0], w["attn_k_norm"][0]]),
        "wr": rank.reshape(KC, P, 2 * GLA_RANK).transpose(1, 0, 2).reshape(P, -1),
        "gup": np.concatenate([w["gla_w_gate_up_f"][0], w["gla_w_gate_up_b"][0]], axis=1),
        "gatew": gate,
        "rope": rotation(),
    }
    nc = bacc.Bacc("TRN2", target_bir_lowering=False, num_devices=1)
    sent, args = {}, []
    for name, a in arrays.items():
        a = np.ascontiguousarray(a)
        sent[f"in_{name}_dram"] = a
        args.append(nc.dram_tensor(f"in_{name}_dram", a.shape, mybir.dt.from_np(a.dtype), kind="ExternalInput").ap())
    out = nc.dram_tensor("out_dram", (1, S, D), mybir.dt.float32, kind="ExternalOutput").ap()
    two_block_kernel(nc, *args, out)
    r = run_bass_kernel_spmd(nc, [sent], core_ids=[0])
    return r.results[0]["out_dram"]
```

```python
import math
from contextlib import ExitStack

import numpy as np

import concourse.bass as bass
from concourse import mybir

P = 128
D = 1024
S = 256
T = S // P
KC = D // P
EPS = 1e-6
GLA_HEADS, GLA_DK, GLA_DV, GLA_RANK, CHUNK = 4, 128, 256, 16, 64
GLA_KEYS = GLA_HEADS * GLA_DK
GATE_NORM = 16.0
Q_HEADS, KV_HEADS, HD = 8, 2, 128
GROUP = Q_HEADS // KV_HEADS
D_FF = 2816
WIDTH = 1536
LRU_HEADS = WIDTH // P
LRU_C = 8.0

UNIT = 2048
RAW = 3
RING = 6
FFN_ITERS = D_FF // 256
LRU_ITERS = LRU_HEADS // 2
SC_ITERS = WIDTH // P
U_Q, U_K, U_V, U_G, U_GO = 0, 2, 4, 8, 12
U_FFN = [16, 59]
FFN_UNITS = 3 * FFN_ITERS
U_KV = U_FFN[0] + FFN_UNITS
U_AQ, U_AO = U_KV + 2, U_KV + 6
assert U_AO + 4 == U_FFN[1]
U_LRU = U_FFN[1] + FFN_UNITS
U_SC = U_LRU + 3 * LRU_ITERS
UNITS = U_SC + 3 * SC_ITERS


def sc_half(u):
    n = u - U_SC
    return n == 3 * SC_ITERS - 1 or (n >= 2 and (n - 2) % 3 == 2)


NORMS = ["mix0", "turn", "ffn0", "mix1", "ffn1", "lru", "sc"]
C_GAMMA = {n: KC * i for i, n in enumerate(NORMS)}
C_FFN = [KC * len(NORMS) + i * 8 * D_FF // P for i in range(2)]
C_GB = C_FFN[1] + 8 * D_FF // P
C_LCONV = C_GB + 2 * GLA_HEADS
C_LGB = C_LCONV + 5 * LRU_HEADS
C_LAM = C_LGB + 2 * LRU_HEADS
C_SCONV = C_LAM + LRU_HEADS
N_PAR = C_SCONV + 3 * SC_ITERS
R_FINAL, R_QN, R_KN = 0, D, D + HD
N_ROW = R_KN + HD

def generations():
    g, f, first, full = 0, 0, {}, {}
    stages = [("norm_mix0", 4, 4), ("rank", 1, 1), ("q", 2, 0), ("k", 2, 0), ("z", 4, 4),
              ("att", 2 * GLA_HEADS, 2 * GLA_HEADS), ("o", 0, 2 * T), ("norm_turn", 4, 4),
              ("norm_ffn0", 4, 4), ("ffn0", 2 * FFN_ITERS, 0),
              ("norm_mix1", 4, 4), ("kv", 2, 0), ("kT", 1, 1), ("qT", 4, 4),
              ("norm_ffn1", 4, 4), ("ffn1", 2 * FFN_ITERS, 0),
              ("norm_lru", 4, 4), ("lru", 0, 2 * LRU_ITERS),
              ("norm_sc", 4, 4), ("sc", 2 * SC_ITERS, 0)]
    for name, banks, signals in stages:
        first[name], full[name] = g, f + 1
        g, f = g + banks, f + signals
    return first, full


GEN, FULL = generations()


def lru_plan():
    units, u = {}, U_LRU
    for j in range(LRU_ITERS + 2):
        for kind, e in (("x", j), ("g", j), ("d", j - 2)):
            if 0 <= e < LRU_ITERS:
                units[kind, e] = u
                u += 1
    assert u == U_SC
    return units


def up_unit(base, e, k):
    return base + k if e == 0 else base + 3 * e - 1 + k


LRU_UNIT = lru_plan()
BRANCH_BANK, GATE_BANK, *HEAD_BANKS = ((GEN["norm_lru"] + n) % 4 for n in range(4))
SCORE_BANKS = [GEN["qT"] % 4, (GEN["qT"] + 1) % 4]
TURNED_BANKS = [(GEN["qT"] + 2) % 4, (GEN["qT"] + 3) % 4]
LRU_AHEAD = [([5], [6], [7]), ([8], [9], []), ([10], [11], [12]), ([13], [14], [15]), ([16], [17], [18]),
             ([], [], []), ([], [], [])]
LRU_AHEAD = [[[U_LRU + u for u in units] for units in step] for step in LRU_AHEAD]

FREED = {"ffn0": 1, "mix1": 2, "ao": 3, "ffn1": 4, "lru": 5, "sc": 6, "final": 7}
LAYERS = ["ffn0", "mix1", "ffn1", "lru", "sc", "final"]
XN = {"mix0": 0, "gla": 2, "ffn0": 4, "mix1": 6, "ffn1": 8, "lru": 10, "sc": 12}
HH = {"mix0": 0, "turn": 4, "ffn0": 8, "mix1": 12, "heads": 16, "ffn1": 24, "lru": 28, "sc": 32}
N_CONSTS = 3
STEP_FFN = [0, FFN_ITERS]
STEP_LRU = 2 * FFN_ITERS
STEP_SC = STEP_LRU + LRU_ITERS
RMS = {"mix0": 0, "gla": 2, "ffn0": 4, "mix1": 6, "k": 8, "q": 9, "ffn1": 11, "lru": 13, "sc": 15, "final": 17}
SUMS = {"mix0": 0, "gla": 4, "ffn0": 6, "mix1": 10, "ffn1": 14, "lru": 18, "sc": 22, "final": 26}


class Chain:

    def __init__(self, eng, sem):
        self.eng, self.sem, self.n, self.per, self.i = eng, sem, 0, 0, 0

    def mark(self, ins):
        ins.then_inc(self.sem, 1)
        self.n += 1

    def wait(self):
        self.eng.wait_ge(self.sem, self.n + self.per * self.i)

    def enter(self, per, i):
        self.per, self.i, self.start = per, i, self.n

    def leave(self, trips):
        assert self.n - self.start == self.per, (self.n - self.start, self.per)
        self.n, self.per, self.i = self.start + self.per * trips, 0, 0


def two_block_kernel(nc, x_in, stream, par_in, row_in, wr_in, gup_in, gatew_in, rope_in, out):
    f32, f32r, u32 = mybir.dt.float32, mybir.dt.float32r, mybir.dt.uint32
    ALU, ACT, AX = mybir.AluOpType, mybir.ActivationFunctionType, mybir.AxisListType

    ctx = ExitStack()
    with ctx:
        def sem(name):
            return ctx.enter_context(nc.semaphore(name))

        top = (nc.sbuf_base + 63) // 64 * 64

        def put(name, shape, dt=f32, at=None):
            nonlocal top
            offset = top if at is None else at
            if at is None:
                top += (4 * int(np.prod(shape[1:])) + 31) // 32 * 32
            return nc.alloc_sbuf_tensor_at(name, shape, dt, offset=offset)

        raw = put("raw", [P, RAW, UNIT])
        w_hi = put("w_hi", [P, RING, UNIT], f32r)
        w_lo = put("w_lo", [P, RING, UNIT], f32r)
        x = put("x", [P, T, D])
        h_at = top
        h_hi = put("h_hi", [P, KC, S], f32r)
        h_lo = put("h_lo", [P, KC, S], f32r)
        par = put("par", [P, N_PAR])
        row = put("row", [P, N_ROW])
        wr = put("wr", [P, KC, 2 * GLA_RANK])
        gup = put("gup", [2 * GLA_RANK, 2, GLA_KEYS])
        rope = put("rope", [P, T, 2, HD])
        ident = put("ident", [P, P])
        causal = put("causal", [P, T, P])
        chunk_on = put("chunk_on", [P, S])
        zeros = put("zeros", [P, 512], f32r)
        power = put("power", [P, 20])
        rt = put("rt", [2 * GLA_RANK, S])
        half_mean = put("half_mean", [P, T])
        stat, mean, rstd = (put(n, [P, 20]) for n in ("stat", "mean", "rstd"))
        sp4, sp8, lam_e, lam_s, lam_q, lam_p = (put(n, [P, LRU_HEADS]) for n in ("sp4", "sp8", "lam_e", "lam_s", "lam_q", "lam_p"))
        xn_at = top
        xn = put("xn", [P, T, D])
        a_hi = put("a_hi", [P, 2, 2, S], f32r)
        a_lo = put("a_lo", [P, 2, 2, S], f32r)
        stage_at = top
        gatew_at = nc.sbuf_usable_end // 64 * 64 - 4 * LRU_HEADS * 2 * P
        gatew = put("gatew", [P, LRU_HEADS, 2 * P], at=gatew_at)

        def stage(at, end, *buffers):
            made = []
            for name, shape in buffers:
                made.append(put(name, shape, at=at))
                at += (4 * int(np.prod(shape[1:])) + 31) // 32 * 32
            assert at <= end, (buffers[0][0], at - end)
            return made

        sbuf_end = nc.sbuf_usable_end
        v, qT, kT, la = stage(stage_at, sbuf_end, ("v", [P, T, D]), ("qT", [P, GLA_HEADS, S]),
                              ("kT", [P, GLA_HEADS, S]), ("la", [P, 2, GLA_HEADS, S]))
        wr_hi = put("wr_hi", [P, KC, 2 * GLA_RANK], f32r, at=stage_at)
        wr_lo = put("wr_lo", [P, KC, 2 * GLA_RANK], f32r, at=stage_at + 4 * KC * 2 * GLA_RANK)
        lt, = stage(xn_at, stage_at, ("lt", [P, 2, GLA_HEADS, S]))
        ep, en, ed, dd, qd, ki, kd, qt, kt = stage(
            xn_at, stage_at, *((n, [P, 2, S]) for n in ("ep", "en", "ed", "dd", "qd", "ki", "kd")),
            ("qt", [P, 2, P]), ("kt", [P, 2, P]))
        sg = put("sg", [P, T, D], at=h_at + 4 * KC * S)
        cacc, sgl, actf = stage(stage_at, gatew_at, ("cacc", [P, 2, 2, S]), ("sgl", [P, 2, S]), ("actf", [P, 2, S]))
        qT2, qr, kv, kr, kT2, pos, neg = stage(
            stage_at, sbuf_end, ("qT2", [P, Q_HEADS, S]), ("qr", [P, T, D]), ("kv", [P, T, 2 * KV_HEADS * HD]),
            ("kr", [P, T, KV_HEADS * HD]), ("kT2", [P, KV_HEADS, S]),
            ("pos", [P, T, Q_HEADS]), ("neg", [P, T, Q_HEADS]))
        rtmp, tabs, nb, sm, mx = stage(xn_at + 4 * D, stage_at, ("rtmp", [P, D]), ("tabs", [P, 2, 2, T, HD]),
                                   ("nb", [P, 2, T]), ("sm", [P, 2, T]), ("mx", [P, 2, T]))
        sq = put("sq", [P, D], at=xn_at)
        pt = put("pt", [P, 2, T, S], at=xn_at)
        kn = put("kn", [P, T, KV_HEADS * HD], at=xn_at + 4 * D + 2 * D)
        pm = put("pm", [P, 2, T, S], at=xn_at + 4 * D)
        xc, gg, rg, ig, ug, iu = stage(stage_at, gatew_at, *((n, [P, 2, S]) for n in ("xc", "gg", "rg", "ig", "ug", "iu")))
        xb, sgate, su, aa = stage(xn_at, xn_at + 4 * T * D, *((n, [P, 2, S]) for n in ("xb", "sgate", "su", "aa")))
        yy, actl = ig, iu
        cgs, pp, ct, sgs, ys, acts = stage(stage_at, gatew_at, *((n, [P, S]) for n in ("cgs", "pp", "ct", "sgs", "ys", "acts")))

        ring = ctx.enter_context(nc.psum_tensor("ring", [P, 4, 512], f32))
        acc = ctx.enter_context(nc.psum_tensor("acc", [P, T, D], f32))

        x_loaded = [sem(f"x_loaded{t}") for t in range(T)]
        consts_loaded, gatew_loaded = sem("consts_loaded"), sem("gatew_loaded")
        rows_loaded = sem("rows_loaded")
        bank_done = sem("bank_done")
        half_added = sem("half_added")
        wr_hi_ready, wr_lo_ready = sem("wr_hi_ready"), sem("wr_lo_ready")
        raw_loaded = [sem(f"raw_loaded{s}") for s in range(RAW)]
        hi_split = sem("hi_split")
        lo_split = sem("lo_split")
        used = sem("used")
        filled = sem("filled")
        ring_free = sem("ring_free")
        acc_free = [sem(f"acc_free{t}") for t in range(T)]
        sumsq = sem("sumsq")
        head_sumsq = sem("head_sumsq")
        rms_ready = sem("rms_ready")
        xn_ready = sem("xn_ready")
        h_hi_ready = sem("h_hi_ready")
        made = sem("made")
        tables_ready = sem("tables_ready")
        z_abs, soft_ready, scan_ready = sem("z_abs"), sem("soft_ready"), sem("scan_ready")
        dd_ready, exps_ready, prod_ready = sem("dd_ready"), sem("exps_ready"), sem("prod_ready")
        v_ready, sg_ready = sem("v_ready"), sem("sg_ready")
        taps_ready = sem("taps_ready")
        gate_ready = sem("gate_ready")
        act_ready = sem("act_ready")
        a_hi_ready, a_lo_ready = sem("a_hi_ready"), sem("a_lo_ready")
        q_tile = sem("q_tile")
        q_read = sem("q_read")
        sq_ready, roped = sem("sq_ready"), sem("roped")
        scale_ready = sem("scale_ready")
        nb_ready, exp_ready = sem("nb_ready"), sem("exp_ready")
        scores_ready = sem("scores_ready")
        probs_ready = sem("probs_ready")
        probs_turned = sem("probs_turned")
        pt_ready = sem("pt_ready")
        o_ready, o_free = sem("o_ready"), sem("o_free")
        lam_ready, sp4_ready = sem("lam_ready"), sem("sp4_ready")
        ri_ready, tanh_ready, decay_ready, sqrt_ready = (sem(n) for n in ("ri_ready", "tanh_ready", "decay_ready", "sqrt_ready"))
        cg_ready = sem("cg_ready")
        branch_free = sem("branch_free")
        conv_ready = sem("conv_ready")
        gate_free = sem("gate_free")
        branch_used = sem("branch_used")
        out_ready, out_stored = sem("out_ready"), sem("out_stored")
        act_own, dve_own, pool_own = sem("act_own"), sem("dve_own"), sem("pool_own")

        block = ctx.enter_context(nc.Block())

        @block.sync
        def _(sp):
            def load(u, i=0, half=False):
                n = UNIT // 2 if half else UNIT
                src = stream[bass.ds(u + 3 * i, 1), :, 0:n].rearrange("o p n -> (o p) n")
                sp.dma_start(raw[:, u % RAW, 0:n], src).then_inc(raw_loaded[u % RAW], 16)

            for t in range(T):
                sp.dma_start(x[:, t, :], x_in[0, t * P:(t + 1) * P, :]).then_inc(x_loaded[t], 16)
            sp.dma_start(par[:, :], par_in).then_inc(consts_loaded, 16)
            sp.dma_start(wr[:, :, :], wr_in.rearrange("p (c n) -> p c n", c=KC)).then_inc(consts_loaded, 16)
            sp.dma_start(gup[:, :, :], gup_in.rearrange("r (a n) -> r a n", a=2)).then_inc(consts_loaded, 16)
            for u in range(RAW):
                load(u)
            whole = (U_SC + 2 - RAW) // RAW
            with sp.Fori(0, whole) as i:
                for k in range(RAW):
                    sp.wait_ge(lo_split, RAW * i + k + 1)
                    load(RAW + k, i)
            for u in range(RAW + RAW * whole, U_SC + 2):
                sp.wait_ge(lo_split, u - RAW + 1)
                load(u)
            with sp.Fori(0, SC_ITERS - 1) as i:
                for k in range(RAW):
                    sp.wait_ge(lo_split, RAW * i + U_SC + 2 + k - RAW + 1)
                    load(U_SC + 2 + k, i, half=k == 2)
            sp.wait_ge(lo_split, UNITS - RAW)
            load(UNITS - 1, half=True)
            for t in range(T):
                sp.wait_ge(out_ready, t + 1)
                sp.dma_start(out[0, t * P:(t + 1) * P, :], xn[:, t, :]).then_inc(out_stored, 16)
            sp.wait_ge(out_stored, 16 * T)

        @block.gpsimd
        def _(pool):
            own = Chain(pool, pool_own)
            own.mark(nc.gpsimd.memset(power[:, :], -0.5))
            nc.gpsimd.memset(zeros[:, :].bitcast(f32), 0.0).then_inc(made, 1)
            for b in (ident, causal, chunk_on):
                own.mark(nc.gpsimd.memset(b[:, :] if b is not causal else b[:, :, :], 1.0))
            own.wait()
            nc.gpsimd.affine_select(out=ident[:, :], in_=ident[:, :], compare_op=ALU.is_equal, fill=0.0,
                                    base=0, pattern=[[-1, P]], channel_multiplier=1).then_inc(made, 1)
            nc.gpsimd.affine_select(out=causal[:, :, :], in_=causal[:, :, :], compare_op=ALU.is_ge, fill=0.0,
                                    base=0, pattern=[[0, T], [1, P]], channel_multiplier=-1).then_inc(made, 1)
            nc.gpsimd.affine_select(out=chunk_on[:, :].rearrange("p (c n) -> p c n", n=CHUNK),
                                    in_=chunk_on[:, :].rearrange("p (c n) -> p c n", n=CHUNK),
                                    compare_op=ALU.is_gt, fill=0.0, base=0,
                                    pattern=[[0, S // CHUNK], [1, CHUNK]], channel_multiplier=0).then_inc(made, 1)

            def rms(first, n, width):
                own.mark(nc.gpsimd.tensor_scalar(mean[:, first:first + n], stat[:, first:first + n],
                                                 1.0 / width, EPS, ALU.mult, ALU.add))
                own.wait()
                nc.gpsimd.tensor_tensor(rstd[:, first:first + n], mean[:, first:first + n],
                                        power[:, first:first + n], ALU.pow).then_inc(rms_ready, 1)

            def rms_of_x(name):
                for t in range(T):
                    pool.wait_ge(sumsq, SUMS[name] + 2 * t + 1)
                    own.mark(nc.gpsimd.tensor_scalar(half_mean[:, t:t + 1], stat[:, 2 * t:2 * t + 1], EPS, None, ALU.add))
                    own.wait()
                    pool.wait_ge(sumsq, SUMS[name] + 2 * t + 2)
                    own.mark(nc.gpsimd.tensor_tensor(mean[:, t:t + 1], stat[:, 2 * t + 1:2 * t + 2], half_mean[:, t:t + 1], ALU.add))
                    own.wait()
                    nc.gpsimd.tensor_tensor(rstd[:, t:t + 1], mean[:, t:t + 1], power[:, t:t + 1], ALU.pow).then_inc(rms_ready, 1)

            rms_of_x("mix0")
            pool.dma_start(row[:, :], row_in.partition_broadcast(P)).then_inc(rows_loaded, 16)
            pool.dma_start(rope[:, :, :, :], rope_in.rearrange("p (t a n) -> p t a n", t=T, a=2)).then_inc(rows_loaded, 16)
            for t in range(T):
                pool.wait_ge(sumsq, SUMS["gla"] + t + 1)
                rms(GLA_HEADS * t, GLA_HEADS, GLA_DV)
            rms_of_x("ffn0")
            rms_of_x("mix1")
            pool.wait_ge(filled, FULL["norm_mix1"] + 3)
            pool.wait_ge(rows_loaded, 32)
            for n, r in ((0, R_QN), (1, R_KN)):
                def weight(a, m):
                    return row[:, a:a + m].unsqueeze(1).to_broadcast([P, T, m])
                half = HD // 2
                nc.gpsimd.tensor_tensor(tabs[:, n, 0, :, :], rope[:, :, 0, :], weight(r, HD), ALU.mult).then_inc(tables_ready, 1)
                nc.gpsimd.tensor_tensor(tabs[:, n, 1, :, 0:half], rope[:, :, 1, 0:half], weight(r + half, half),
                                        ALU.mult).then_inc(tables_ready, 1)
                nc.gpsimd.tensor_tensor(tabs[:, n, 1, :, half:HD], rope[:, :, 1, half:HD], weight(r, half),
                                        ALU.mult).then_inc(tables_ready, 1)
            pool.wait_ge(head_sumsq, 1)
            rms(16, T * KV_HEADS, HD)
            for t in range(T):
                pool.wait_ge(head_sumsq, t + 2)
                rms(Q_HEADS * t, Q_HEADS, HD)
                pool.wait_ge(rms_ready, RMS["q"] + t + 1)
                for buf, sign in ((pos, 1), (neg, -1)):
                    nc.gpsimd.tensor_scalar(buf[:, t, :], rstd[:, Q_HEADS * t:Q_HEADS * (t + 1)], sign * HD ** -0.5, None,
                                            ALU.mult).then_inc(scale_ready, 1)
            rms_of_x("ffn1")
            pool.dma_start(gatew[:, :, :], gatew_in.rearrange("p (h n) -> p h n", h=LRU_HEADS)).then_inc(gatew_loaded, 16)
            rms_of_x("lru")
            rms_of_x("sc")
            rms_of_x("final")

        @block.scalar
        def _(act):
            own = Chain(act, act_own)

            def split(u, i=0, half=False):
                n = UNIT // 2 if half else UNIT
                act.wait_ge(raw_loaded[u % RAW], 16 * (u // RAW + 1) + 16 * (RING // RAW) * i)
                if u >= RING:
                    act.wait_ge(used, u - RING + 1 + RING * i)
                nc.scalar.activation(w_hi[:, u % RING, 0:n], raw[:, u % RAW, 0:n], ACT.Copy).then_inc(hi_split, 1)

            def sums(t, name):
                for half in range(2):
                    if name != "mix0":
                        act.wait_ge(*((half_added, T * LAYERS.index(name) + t + 1), (acc_free[t], FREED[name]))[half])
                    at = slice(half * 512, (half + 1) * 512)
                    nc.scalar.activation(xn[:, t, at], x[:, t, at], ACT.Square, scale=D ** -0.5,
                                         accum_out=stat[:, 2 * t + half:2 * t + half + 1]).then_inc(sumsq, 1)

            def turned(name):
                for b in range(4):
                    act.wait_ge(filled, FULL["norm_" + name] + b)
                    for k in range(2):
                        kc = 2 * b + k
                        last = nc.scalar.activation(h_hi[:, kc, :], ring[:, (GEN["norm_" + name] + b) % 4, k * S:(k + 1) * S],
                                                    ACT.Copy, scale=par[:, C_GAMMA[name] + kc:C_GAMMA[name] + kc + 1])
                    last.then_inc(h_hi_ready, 1)

            for t in range(T):
                act.wait_ge(x_loaded[t], 16)
                sums(t, "mix0")
            act.wait_ge(consts_loaded, 16 * N_CONSTS)
            nc.scalar.activation(wr_hi[:, :, :], wr[:, :, :], ACT.Copy).then_inc(wr_hi_ready, 1)
            turned("mix0")
            split(0)
            split(1)
            own.mark(nc.scalar.activation(lam_p[:, :], par[:, C_LAM:C_LAM + LRU_HEADS], ACT.Abs))
            own.wait()
            nc.scalar.activation(lam_e[:, :], lam_p[:, :], ACT.Exp, scale=-1.0).then_inc(lam_ready, 1)
            for u in range(2, 6):
                split(u)
            for d in range(2):
                for b in range(2):
                    g = GEN["z"] + 2 * d + b
                    act.wait_ge(filled, FULL["z"] + 2 * d + b)
                    for k in range(2):
                        h = 2 * b + k
                        c = C_GB + GLA_HEADS * d + h
                        last = nc.scalar.activation(lt[:, d, h, :], ring[:, g % 4, k * S:(k + 1) * S], ACT.Abs,
                                                    bias=par[:, c:c + 1])
                        own.mark(last) if k == 0 else last.then_inc(z_abs, 1)
                split(6 + d)
            act.wait_ge(z_abs, 4)
            own.wait()
            for d in range(2):
                own.mark(nc.scalar.activation(lt[:, d, :, :], lt[:, d, :, :], ACT.Exp, scale=-1.0))
            own.wait()
            for d in range(2):
                nc.scalar.activation(lt[:, d, :, :], lt[:, d, :, :], ACT.Ln, bias=1.0).then_inc(soft_ready, 1)
            split(8)

            def exps(h):
                act.wait_ge(dd_ready, h + 1)
                if h:
                    act.wait_ge(prod_ready, h)
                nc.scalar.activation(ep[:, :, :], la[:, :, h, :], ACT.Exp, scale=1.0 / GATE_NORM).then_inc(exps_ready, 1)
                nc.scalar.activation(en[:, :, :], la[:, :, h, :], ACT.Exp, scale=-1.0 / GATE_NORM).then_inc(exps_ready, 1)
                nc.scalar.activation(ed[:, :, :], dd[:, :, :], ACT.Exp, scale=1.0 / GATE_NORM).then_inc(exps_ready, 1)

            exps(0)
            split(9)
            act.wait_ge(used, U_V + 4)
            for t in range(T):
                nc.scalar.activation(v[:, t, :], acc[:, t, :], ACT.Copy).then_inc(v_ready, 1)
            for h in range(1, GLA_HEADS):
                exps(h)
                split(9 + h)
            split(13)
            split(14)
            act.wait_ge(used, U_G + 4)
            for t in range(T):
                nc.scalar.activation(sg[:, t, :], acc[:, t, :], ACT.Silu).then_inc(sg_ready, 1)
            split(15)
            for t in range(T):
                for h in range(GLA_HEADS):
                    if h % 2 == 0:
                        act.wait_ge(filled, FULL["o"] + 2 * t + h // 2)
                    c = GLA_HEADS * t + h
                    last = nc.scalar.activation(xn[:, t, h * GLA_DV:(h + 1) * GLA_DV], acc[:, t, h * GLA_DV:(h + 1) * GLA_DV],
                                                ACT.Square, accum_out=stat[:, c:c + 1])
                    own.mark(last) if h < GLA_HEADS - 1 else last.then_inc(sumsq, 1)
            turned("turn")
            split(16)
            split(17)

            def ffn(n):
                B, G, C, J = U_FFN[n], GEN[f"ffn{n}"], C_FFN[n], STEP_FFN[n]

                def taps(e, i, k):
                    act.wait_ge(used, up_unit(B, e, k) + 1 + 6 * i)
                    for half in range(2):
                        c = C + 8 * (2 * e + k) + 4 * half + 32 * i
                        last = nc.scalar.activation(cacc[:, k, half, :], ring[:, (G + 2 * e + k) % 4, half * S:(half + 1) * S],
                                                    ACT.Identity, scale=par[:, bass.ds(c + 1, 1)], bias=par[:, bass.ds(c + 3, 1)])
                    last.then_inc(taps_ready, 1)

                def step(e, i=0, last=False):
                    taps(e, i, 0)
                    split(B + 5 + 3 * e, i)
                    taps(e, i, 1)
                    act.wait_ge(ring_free, G + 2 * e + 2 + 4 * i)
                    nc.scalar.activation(sgl[:, :, :], cacc[:, :, 1, :], ACT.Silu).then_inc(gate_ready, 1)
                    act.wait_ge(act_ready, J + e + 1 + 2 * i)
                    act.wait_ge(used, B + 3 * e - 1 + 6 * i)
                    nc.scalar.activation(a_hi[:, e % 2, :, :], actf[:, :, :], ACT.Copy).then_inc(a_hi_ready, 1)
                    if not last:
                        split(B + 6 + 3 * e, i)
                        split(B + 7 + 3 * e, i)

                step(0)
                with act.Fori(0, FFN_ITERS // 2 - 1) as i:
                    for e in (1, 2):
                        step(e, i)
                step(FFN_ITERS - 2)
                step(FFN_ITERS - 1, last=True)

            for u in range(18, 20):
                split(u)
            for t in range(T):
                sums(t, "ffn0")
            turned("ffn0")
            split(20)
            ffn(0)

            for t in range(T):
                sums(t, "mix1")
            turned("mix1")
            for u in range(U_KV + 3, U_KV + 6):
                split(u)
            act.wait_ge(ring_free, GEN["kv"] + 2)
            nc.scalar.activation(sq[:, 0:T * KV_HEADS * HD].rearrange("p (t n) -> p t n", t=T), kv[:, :, 0:KV_HEADS * HD],
                                 ACT.Square).then_inc(sq_ready, 1)
            split(U_AO)
            split(U_AO + 1)
            for t in range(T):
                if t == 0:
                    act.wait_ge(q_tile, 1)
                else:
                    act.wait_ge(used, U_AQ + 4)
                act.wait_ge(head_sumsq, t + 1)
                nc.scalar.activation(sq[:, 512:D], acc[:, t, 512:D], ACT.Square).then_inc(sq_ready, 1)
                act.wait_ge(q_read, t + 1)
                nc.scalar.activation(sq[:, 0:512], acc[:, t, 0:512], ACT.Square).then_inc(sq_ready, 1)
                if t == 0:
                    split(U_AO + 2)
                    split(U_AO + 3)
            act.wait_ge(scale_ready, 2 * T)
            for h in range(Q_HEADS + 4):
                e = h - 3
                if 0 <= e < Q_HEADS:
                    act.wait_ge(probs_turned, e + 1)
                    nc.scalar.activation(pt[:, e % 2, :, :], ring[:, TURNED_BANKS[e % 2], :].rearrange("p (k s) -> p k s", k=2),
                                         ACT.Copy).then_inc(pt_ready, 1)
                e = h - 4
                if e >= 0:
                    act.wait_ge(o_ready, e + 1)
                    nc.scalar.activation(h_hi[:, e, :], acc[:, 0, (e % 2) * 512:(e % 2) * 512 + S],
                                         ACT.Copy).then_inc(h_hi_ready, 1)
                if h < Q_HEADS:
                    act.wait_ge(nb_ready, h + 1)
                    if h >= 2:
                        act.wait_ge(probs_turned, h - 1)
                    for t in range(T):
                        nc.scalar.activation(pm[:, h % 2, t, :], ring[:, SCORE_BANKS[h % 2], t * S:(t + 1) * S], ACT.Exp,
                                             bias=nb[:, h % 2, t:t + 1], scale=pos[:, t, h:h + 1],
                                             accum_out=sm[:, h % 2, t:t + 1]).then_inc(exp_ready, 1)
            for u in range(U_AO + 4, U_AO + 8):
                split(u)
            for t in range(T):
                sums(t, "ffn1")
            turned("ffn1")
            split(U_FFN[1] + 4)
            ffn(1)

            for t in range(T):
                sums(t, "lru")
            turned("lru")
            split(U_LRU + 3)
            split(U_LRU + 4)
            for j in range(LRU_ITERS + 1):
                e, plan = j - 1, LRU_AHEAD[j]
                if j < LRU_ITERS:
                    act.wait_ge(used, LRU_UNIT["x", j] + 1)
                    if j:
                        act.wait_ge(conv_ready, j)
                    nc.scalar.activation(xb[:, :, :], ring[:, BRANCH_BANK, :].rearrange("p (k s) -> p k s", k=2),
                                         ACT.Copy).then_inc(branch_free, 1)
                if j:
                    for k in range(2):
                        act.wait_ge(filled, FULL["lru"] + 2 * e + k)
                        for r, buf in ((0, rg), (1, ig)):
                            c = C_LGB + 2 * (2 * e + k) + r
                            last = nc.scalar.activation(buf[:, k, :], ring[:, HEAD_BANKS[k], r * S:(r + 1) * S],
                                                        ACT.Sigmoid, bias=par[:, c:c + 1])
                            own.mark(last) if r == 0 else last.then_inc(ri_ready, 1)
                    own.wait()
                    if e == 0:
                        act.wait_ge(sp4_ready, 1)
                    for k in range(2):
                        h = 2 * e + k
                        nc.scalar.activation(ug[:, k, :], rg[:, k, :], ACT.Tanh, scale=sp4[:, h:h + 1]).then_inc(tanh_ready, 1)
                if j < LRU_ITERS:
                    if j:
                        act.wait_ge(branch_used, j)
                    act.wait_ge(branch_free, j + 1)
                    for k in range(2):
                        c = C_LCONV + 5 * (2 * j + k)
                        last = nc.scalar.activation(xc[:, k, :], xb[:, k, :], ACT.Identity,
                                                    scale=par[:, c + 3:c + 4], bias=par[:, c + 4:c + 5])
                    last.then_inc(taps_ready, 1)
                if j:
                    for k in range(2):
                        h = 2 * e + k
                        nc.scalar.activation(aa[:, k, :], rg[:, k, :], ACT.Exp, scale=sp8[:, h:h + 1]).then_inc(decay_ready, 1)
                    act.wait_ge(tanh_ready, 2 * e + 2)
                    nc.scalar.activation(su[:, :, :], ug[:, :, :], ACT.Sqrt).then_inc(sqrt_ready, 1)
                for u in plan[0]:
                    split(u)
                if j < LRU_ITERS:
                    act.wait_ge(used, LRU_UNIT["g", j] + 1)
                    if j:
                        act.wait_ge(gate_free, j)
                    nc.scalar.activation(sgate[:, :, :], ring[:, GATE_BANK, :].rearrange("p (k s) -> p k s", k=2),
                                         ACT.Sigmoid).then_inc(gate_ready, 1)
                for u in plan[1]:
                    split(u)
                if j:
                    act.wait_ge(act_ready, STEP_LRU + e + 1)
                    act.wait_ge(used, LRU_UNIT["d", e - 2] + 1 if e >= 2 else U_LRU)
                    nc.scalar.activation(a_hi[:, e % 2, :, :], actl[:, :, :], ACT.Copy).then_inc(a_hi_ready, 1)
                for u in plan[2]:
                    split(u)

            for t in range(T):
                sums(t, "sc")
            turned("sc")
            for u in range(U_SC + 1, U_SC + 4):
                split(u)
            split(U_SC + 4, half=True)

            def sc_step(e, i=0, splits=3):
                act.wait_ge(used, up_unit(U_SC, e, 0) + 1 + 6 * i)
                nc.scalar.activation(cgs[:, :], ring[:, (GEN["sc"] + 2 * e) % 4, 0:S], ACT.Copy).then_inc(cg_ready, 1)
                act.wait_ge(used, up_unit(U_SC, e, 1) + 1 + 6 * i)
                nc.scalar.activation(sgs[:, :], ring[:, (GEN["sc"] + 2 * e + 1) % 4, S:2 * S], ACT.Silu).then_inc(gate_ready, 1)
                for k in range(splits):
                    if k == 1:
                        ahead(e, i)
                    split(U_SC + 5 + 3 * e + k, i, half=sc_half(U_SC + 5 + 3 * e + k))
                if splits < 2:
                    ahead(e, i)
                act.wait_ge(act_ready, STEP_SC + e + 1 + 2 * i)
                act.wait_ge(used, U_SC + 3 * e - 1 + 6 * i)
                nc.scalar.activation(a_hi[:, e % 2, 0, :], acts[:, :], ACT.Copy).then_inc(a_hi_ready, 1)

            def ahead(e, i):
                c = C_SCONV + 3 * e + 6 * i
                act.wait_ge(ring_free, GEN["sc"] + 2 * e + 1 + 4 * i)
                nc.scalar.activation(ct[:, :], pp[:, :], ACT.Identity, scale=par[:, bass.ds(c + 2, 1)], bias=0.0).then_inc(taps_ready, 1)

            sc_step(0)
            with act.Fori(0, (SC_ITERS - 4) // 2) as i:
                for e in (1, 2):
                    sc_step(e, i)
            sc_step(SC_ITERS - 3)
            sc_step(SC_ITERS - 2, splits=1)
            sc_step(SC_ITERS - 1, splits=0)
            for t in range(T):
                sums(t, "final")

        @block.vector
        def _(dve):
            own = Chain(dve, dve_own)

            def split(u, i=0, half=False):
                n = UNIT // 2 if half else UNIT
                dve.wait_ge(hi_split, u + 1 + RING * i)
                nc.vector.tensor_tensor(w_lo[:, u % RING, 0:n], raw[:, u % RAW, 0:n], w_hi[:, u % RING, 0:n].bitcast(f32),
                                        ALU.subtract).then_inc(lo_split, 1)

            def normed(name):
                for t in range(T):
                    dve.wait_ge(rms_ready, RMS[name] + t + 1)
                    nc.vector.tensor_scalar(xn[:, t, :], x[:, t, :], rstd[:, t:t + 1], None, ALU.mult).then_inc(xn_ready, 1)

            def turned(name):
                for b in range(4):
                    dve.wait_ge(h_hi_ready, HH[name] + b + 1)
                    for k in range(2):
                        kc = 2 * b + k
                        c = C_GAMMA[name] + kc
                        last = nc.vector.scalar_tensor_tensor(
                            out=h_lo[:, kc, :], in0=ring[:, (GEN["norm_" + name] + b) % 4, k * S:(k + 1) * S],
                            scalar=par[:, c:c + 1], in1=h_hi[:, kc, :].bitcast(f32), op0=ALU.mult, op1=ALU.subtract)
                    last.then_inc(ring_free, 1)

            def residual(layer, units):
                for t in range(T):
                    for half in range(2):
                        if (t, half) != (T - 1, 1):
                            dve.wait_ge(bank_done, (2 * T - 1) * (layer - 1) + 2 * t + half + 1)
                        else:
                            dve.wait_ge(used, units)
                        at = slice(half * 512, (half + 1) * 512)
                        nc.vector.tensor_tensor(x[:, t, at], acc[:, t, at], x[:, t, at], ALU.add).then_inc(
                            (half_added, acc_free[t])[half], 1)

            def two(bank):
                return ring[:, bank % 4, :].rearrange("p (k s) -> p k s", k=2)

            for t in range(T):
                dve.wait_ge(x_loaded[t], 16)
            normed("mix0")
            dve.wait_ge(consts_loaded, 16 * N_CONSTS)
            dve.wait_ge(wr_hi_ready, 1)
            nc.vector.tensor_tensor(wr_lo[:, :, :], wr[:, :, :], wr_hi[:, :, :].bitcast(f32), ALU.subtract).then_inc(wr_lo_ready, 1)
            turned("mix0")
            split(0)
            split(1)
            dve.wait_ge(filled, FULL["rank"])
            nc.vector.tensor_copy(rt[:, :], ring[0:2 * GLA_RANK, GEN["rank"] % 4, 0:S]).then_inc(ring_free, 1)
            split(2)
            split(3)
            for b in range(2):
                dve.wait_ge(used, U_Q + b + 1)
                nc.vector.tensor_scalar(qT[:, 2 * b:2 * b + 2, :], two(GEN["q"] + b), GLA_DK ** -0.5, None,
                                        ALU.mult).then_inc(ring_free, 1)
            split(4)
            for b in range(2):
                dve.wait_ge(used, U_K + b + 1)
                nc.vector.tensor_copy(kT[:, 2 * b:2 * b + 2, :], two(GEN["k"] + b)).then_inc(ring_free, 1)
            split(5)
            for d in range(2):
                for b in range(2):
                    dve.wait_ge(z_abs, 2 * d + b + 1)
                    for k in range(2):
                        h = 2 * b + k
                        c = C_GB + GLA_HEADS * d + h
                        last = nc.vector.tensor_scalar(la[:, d, h, :], ring[:, (GEN["z"] + 2 * d + b) % 4, k * S:(k + 1) * S],
                                                       par[:, c:c + 1], 0.0, ALU.add, ALU.min)
                        own.mark(last) if k == 0 else last.then_inc(ring_free, 1)
                split(6 + d)
            dve.wait_ge(made, 4)
            for d in range(2):
                dve.wait_ge(soft_ready, d + 1)
                own.wait()
                dve.wait_ge(ring_free, GEN["z"] + 4)
                own.mark(nc.vector.tensor_tensor(lt[:, d, :, :], la[:, d, :, :], lt[:, d, :, :], ALU.subtract))
                own.wait()
                for h in range(GLA_HEADS):
                    order = slice(None) if d == 0 else slice(S - 1, None, -1)
                    own.mark(nc.vector.tensor_tensor_scan(out=la[:, d, h, order], data0=chunk_on[:, :], data1=lt[:, d, h, order],
                                                          initial=0.0, op0=ALU.mult, op1=ALU.add))
            own.wait()

            def differences(h):
                for d in range(2):
                    by_chunk = la[:, d, h, :].rearrange("p (c n) -> p c n", n=CHUNK)
                    end = by_chunk[:, :, CHUNK - 1:CHUNK] if d == 0 else by_chunk[:, :, 0:1]
                    last = nc.vector.tensor_tensor(dd[:, d, :].rearrange("p (c n) -> p c n", n=CHUNK),
                                                   end.to_broadcast([P, S // CHUNK, CHUNK]), by_chunk, ALU.subtract)
                    own.mark(last) if d == 0 else last.then_inc(dd_ready, 1)

            def products(h):
                dve.wait_ge(exps_ready, 3 * h + 3)
                for o, e, s in ((qd, ep, qT), (ki, en, kT), (kd, ed, kT)):
                    own.mark(nc.vector.tensor_tensor(o[:, :, :], e[:, :, :], s[:, h:h + 1, :].to_broadcast([P, 2, S]), ALU.mult))
                own.wait()
                C = CHUNK
                own.mark(nc.vector.tensor_scalar(kt[:, 0, 0:C], kd[:, 0, 0:C], ep[:, 0, 2 * C - 1:2 * C], None, ALU.mult))
                own.mark(nc.vector.tensor_copy(kt[:, 0, C:2 * C], kd[:, 0, C:2 * C]))
                own.mark(nc.vector.tensor_copy(qt[:, 0, 0:C], qd[:, 0, 2 * C:3 * C]))
                own.mark(nc.vector.tensor_scalar(qt[:, 0, C:2 * C], qd[:, 0, 3 * C:4 * C], ep[:, 0, 3 * C - 1:3 * C], None, ALU.mult))
                own.mark(nc.vector.tensor_copy(kt[:, 1, 0:C], kd[:, 1, 2 * C:3 * C]))
                own.mark(nc.vector.tensor_scalar(kt[:, 1, C:2 * C], kd[:, 1, 3 * C:4 * C], ep[:, 1, 2 * C:2 * C + 1], None, ALU.mult))
                own.mark(nc.vector.tensor_scalar(qt[:, 1, 0:C], qd[:, 1, 0:C], ep[:, 1, C:C + 1], None, ALU.mult))
                nc.vector.tensor_copy(qt[:, 1, C:2 * C], qd[:, 1, C:2 * C]).then_inc(prod_ready, 1)

            def scores(h):
                g = GEN["att"] + 2 * h
                near, far = (b[:, h, :].rearrange("p (t c) -> p t c", t=T) for b in (qT, kT))
                dve.wait_ge(filled, FULL["att"] + 2 * h)
                own.mark(nc.vector.tensor_copy(near, ring[:, g % 4, T * P:2 * T * P].rearrange("p (t c) -> p t c", t=T)))
                own.wait()
                nc.vector.copy_predicated(near, causal[:, :, :].bitcast(u32),
                                          ring[:, g % 4, 0:T * P].rearrange("p (t c) -> p t c", t=T)).then_inc(ring_free, 1)
                dve.wait_ge(filled, FULL["att"] + 2 * h + 1)
                nc.vector.tensor_copy(far, ring[:, (g + 1) % 4, 0:T * P].rearrange("p (t c) -> p t c", t=T)).then_inc(ring_free, 1)

            differences(0)
            split(8)
            products(0)
            differences(1)
            split(9)
            for h in range(1, GLA_HEADS):
                scores(h - 1)
                products(h)
                if h + 1 < GLA_HEADS:
                    differences(h + 1)
                split(9 + h)
            scores(GLA_HEADS - 1)
            for u in range(13, 16):
                split(u)
            dve.wait_ge(lam_ready, 1)
            own.mark(nc.vector.tensor_scalar(lam_q[:, :], lam_e[:, :], 2.0, None, ALU.add))
            own.wait()
            own.mark(nc.vector.reciprocal(lam_p[:, :], lam_q[:, :]))
            own.wait()
            own.mark(nc.vector.tensor_tensor(lam_s[:, :], lam_e[:, :], lam_p[:, :], ALU.mult))
            own.wait()
            own.mark(nc.vector.tensor_tensor(lam_q[:, :], lam_s[:, :], lam_s[:, :], ALU.mult))
            own.mark(nc.vector.memset(lam_p[:, :], 1.0 / 17))
            for n in (15, 13, 11, 9, 7, 5, 3, 1):
                own.wait()
                own.mark(nc.vector.tensor_tensor(lam_p[:, :], lam_p[:, :], lam_q[:, :], ALU.mult))
                own.wait()
                own.mark(nc.vector.tensor_scalar(lam_p[:, :], lam_p[:, :], 1.0 / n, None, ALU.add))
            own.wait()
            own.mark(nc.vector.tensor_tensor(lam_p[:, :], lam_p[:, :], lam_s[:, :], ALU.mult))
            own.mark(nc.vector.tensor_scalar(lam_q[:, :], par[:, C_LAM:C_LAM + LRU_HEADS], -1.0, 0.0, ALU.mult, ALU.max))
            own.wait()
            own.mark(nc.vector.scalar_tensor_tensor(out=lam_p[:, :], in0=lam_p[:, :], scalar=2.0, in1=lam_q[:, :],
                                                    op0=ALU.mult, op1=ALU.add))
            own.wait()
            own.mark(nc.vector.tensor_scalar(sp8[:, :], lam_p[:, :], -LRU_C, None, ALU.mult))
            nc.vector.tensor_scalar(sp4[:, :], lam_p[:, :], LRU_C / 2, None, ALU.mult).then_inc(sp4_ready, 1)
            for t in range(T):
                dve.wait_ge(rms_ready, RMS["gla"] + t + 1)
                for h in range(GLA_HEADS):
                    at = slice(h * GLA_DV, (h + 1) * GLA_DV)
                    c = GLA_HEADS * t + h
                    last = nc.vector.scalar_tensor_tensor(out=xn[:, t, at], in0=acc[:, t, at], scalar=rstd[:, c:c + 1],
                                                          in1=sg[:, t, at], op0=ALU.mult, op1=ALU.mult)
                    own.mark(last) if h < GLA_HEADS - 1 else last.then_inc(xn_ready, 1)
            turned("turn")
            for u in range(16, 20):
                split(u)
            residual(1, U_GO + 4)

            def ffn(n):
                B, G, C, J = U_FFN[n], GEN[f"ffn{n}"], C_FFN[n], STEP_FFN[n]

                def conv(e, i, k):
                    dve.wait_ge(taps_ready, 2 * J + 2 * e + k + 1 + 4 * i)
                    bank = (G + 2 * e + k) % 4
                    for tap, out_at, in_at in ((0, slice(1, S), slice(0, S - 1)), (2, slice(0, S - 1), slice(1, S))):
                        for half in range(2):
                            c = C + 8 * (2 * e + k) + 4 * half + tap + 32 * i
                            lo = half * S
                            last = nc.vector.scalar_tensor_tensor(
                                out=cacc[:, k, half, out_at], in0=ring[:, bank, lo + in_at.start:lo + in_at.stop],
                                scalar=par[:, bass.ds(c, 1)], in1=cacc[:, k, half, out_at], op0=ALU.mult, op1=ALU.add)
                            if (tap, half) != (2, 1):
                                own.mark(last)
                        if tap == 0:
                            own.wait()
                    last.then_inc(ring_free, 1)

                def step(e, i=0, last=False):
                    conv(e, i, 0)
                    split(B + 5 + 3 * e, i)
                    conv(e, i, 1)
                    dve.wait_ge(gate_ready, J + e + 1 + 2 * i)
                    own.wait()
                    nc.vector.tensor_tensor(actf[:, :, :], cacc[:, :, 0, :], sgl[:, :, :], ALU.mult).then_inc(act_ready, 1)
                    dve.wait_ge(a_hi_ready, J + e + 1 + 2 * i)
                    nc.vector.tensor_tensor(a_lo[:, e % 2, :, :], actf[:, :, :], a_hi[:, e % 2, :, :].bitcast(f32),
                                            ALU.subtract).then_inc(a_lo_ready, 1)
                    if not last:
                        split(B + 6 + 3 * e, i)
                        split(B + 7 + 3 * e, i)

                step(0)
                with dve.Fori(0, FFN_ITERS // 2 - 1) as i:
                    own.enter(12, i)
                    for e in (1, 2):
                        step(e, i)
                own.leave(FFN_ITERS // 2 - 1)
                step(FFN_ITERS - 2)
                step(FFN_ITERS - 1, last=True)

            normed("ffn0")
            turned("ffn0")
            split(20)
            ffn(0)
            residual(2, U_FFN[0] + FFN_UNITS)

            normed("mix1")
            turned("mix1")
            for u in range(U_KV + 3, U_KV + 6):
                split(u)
            dve.wait_ge(used, U_KV + 2)
            for t in range(T):
                nc.vector.tensor_copy(kv[:, t, :], ring[:, (GEN["kv"] + t) % 4, :]).then_inc(ring_free, 1)
            split(U_AO)

            def rotate(o, a, tmp, heads, n, t, freed=None):
                half = HD // 2
                view = a.rearrange("p (h a n) -> p h a n", h=heads, a=2)
                own.mark(nc.vector.tensor_tensor(o.rearrange("p (h n) -> p h n", h=heads), a.rearrange("p (h n) -> p h n", h=heads),
                                                 tabs[:, n, 0, t, :].unsqueeze(1).to_broadcast([P, heads, HD]), ALU.mult))
                for side in range(2):
                    last = nc.vector.tensor_tensor(
                        tmp.rearrange("p (h a n) -> p h a n", h=heads, a=2)[:, :, side, :], view[:, :, 1 - side, :],
                        tabs[:, n, 1, t, side * half:(side + 1) * half].unsqueeze(1).to_broadcast([P, heads, half]), ALU.mult)
                    if side == 1 and freed is not None:
                        last.then_inc(*freed[:1], 1)
                        dve.wait_ge(*freed)
                    else:
                        own.mark(last)
                own.wait()
                return nc.vector.tensor_tensor(o, o, tmp, ALU.add)

            NK = T * KV_HEADS
            dve.wait_ge(sq_ready, 1)
            nc.vector.tensor_reduce(out=stat[:, 16:16 + NK], in_=sq[:, 0:NK * HD].rearrange("p (g n) -> p g n", g=NK),
                                    axis=AX.X, op=ALU.add).then_inc(head_sumsq, 1)
            split(U_AO + 1)
            dve.wait_ge(rms_ready, RMS["k"] + 1)
            dve.wait_ge(tables_ready, 6)
            for t in range(T):
                scale = rstd[:, 16 + t * KV_HEADS:16 + (t + 1) * KV_HEADS].unsqueeze(2).to_broadcast([P, KV_HEADS, HD])
                own.mark(nc.vector.tensor_tensor(kn[:, t, :].rearrange("p (h n) -> p h n", h=KV_HEADS),
                                                 kv[:, t, 0:KV_HEADS * HD].rearrange("p (h n) -> p h n", h=KV_HEADS), scale, ALU.mult))
                own.wait()
                rotate(kr[:, t, :], kn[:, t, :], rtmp[:, t * 256:t * 256 + KV_HEADS * HD], KV_HEADS, 1, t).then_inc(roped, 1)
            dve.wait_ge(roped, T)
            for t in range(T):
                if t == 0:
                    dve.wait_ge(q_tile, 1)
                else:
                    dve.wait_ge(used, U_AQ + 4)
                rotate(qr[:, t, 0:512], acc[:, t, 0:512], rtmp[:, 0:512], Q_HEADS // 2, 0, t, freed=(q_read, t + 1)).then_inc(roped, 1)
                dve.wait_ge(sq_ready, 2 * t + 2)
                rotate(qr[:, t, 512:D], acc[:, t, 512:D], rtmp[:, 512:D], Q_HEADS // 2, 0, t,
                       freed=(acc_free[t], FREED["ao"])).then_inc(roped, 1)
                dve.wait_ge(sq_ready, 2 * t + 3)
                nc.vector.tensor_reduce(out=stat[:, t * Q_HEADS:(t + 1) * Q_HEADS],
                                        in_=sq[:, :].rearrange("p (g n) -> p g n", g=Q_HEADS), axis=AX.X, op=ALU.add).then_inc(head_sumsq, 1)
                dve.wait_ge(roped, T + 2 * t + 2)
                if t == 0:
                    split(U_AO + 2)
                    dve.wait_ge(filled, FULL["kT"])
                    nc.vector.tensor_copy(kT2[:, :, :], two(GEN["kT"])).then_inc(ring_free, 1)
            for b in range(4):
                dve.wait_ge(filled, FULL["qT"] + b)
                nc.vector.tensor_copy(qT2[:, 2 * b:2 * b + 2, :], two(GEN["qT"] + b)).then_inc(ring_free, 1)
            for h in range(Q_HEADS + 4):
                if h < Q_HEADS:
                    dve.wait_ge(scores_ready, h + 1)
                    if h >= 2:
                        dve.wait_ge(probs_ready, h - 1)
                    own.mark(nc.vector.reduce_max(mx[:, h % 2, :], two(SCORE_BANKS[h % 2]), AX.X))
                    if h == 0:
                        dve.wait_ge(scale_ready, 2 * T)
                    own.wait()
                    nc.vector.tensor_tensor(nb[:, h % 2, :], mx[:, h % 2, :], neg[:, :, h], ALU.mult).then_inc(nb_ready, 1)
                e = h - 4
                if e >= 0:
                    dve.wait_ge(h_hi_ready, HH["heads"] + e + 1)
                    nc.vector.tensor_tensor(h_lo[:, e, :], acc[:, 0, (e % 2) * 512:(e % 2) * 512 + S], h_hi[:, e, :].bitcast(f32),
                                            ALU.subtract).then_inc(o_free, 1)
                e = h - 1
                if 0 <= e < Q_HEADS:
                    dve.wait_ge(exp_ready, 2 * e + 2)
                    own.mark(nc.vector.reciprocal(mx[:, e % 2, :], sm[:, e % 2, :]))
                    own.wait()
                    nc.vector.tensor_tensor(pm[:, e % 2, :, :], pm[:, e % 2, :, :], mx[:, e % 2, :].unsqueeze(2).to_broadcast([P, T, S]),
                                            ALU.mult).then_inc(probs_ready, 1)
            for u in range(U_AO + 3, U_AO + 8):
                split(u)
            residual(3, U_AO + 4)
            normed("ffn1")
            turned("ffn1")
            split(U_FFN[1] + 4)
            ffn(1)
            residual(4, U_FFN[1] + FFN_UNITS)

            normed("lru")
            turned("lru")
            split(U_LRU + 3)
            split(U_LRU + 4)
            for j in range(LRU_ITERS + 1):
                e, plan = j - 1, LRU_AHEAD[j]
                if j:
                    dve.wait_ge(ri_ready, 2 * e + 2)
                    own.wait()
                    dve.wait_ge(conv_ready, e + 1)
                    if e:
                        dve.wait_ge(a_lo_ready, STEP_LRU + e)
                    nc.vector.tensor_tensor(iu[:, :, :], ig[:, :, :], xc[:, :, :], ALU.mult).then_inc(branch_used, 1)
                if j < LRU_ITERS:
                    dve.wait_ge(taps_ready, 2 * STEP_LRU + j + 1)
                    for back in (1, 2, 3):
                        for k in range(2):
                            c = C_LCONV + 5 * (2 * j + k) + 3 - back
                            last = nc.vector.scalar_tensor_tensor(
                                out=xc[:, k, back:S], in0=xb[:, k, 0:S - back], scalar=par[:, c:c + 1],
                                in1=xc[:, k, back:S], op0=ALU.mult, op1=ALU.add)
                            if (back, k) != (3, 1):
                                own.mark(last)
                        if back < 3:
                            own.wait()
                    last.then_inc(conv_ready, 1)
                if j:
                    dve.wait_ge(branch_used, e + 1)
                    dve.wait_ge(decay_ready, 2 * e + 2)
                    own.mark(nc.vector.scalar_tensor_tensor(out=iu[:, :, :], in0=aa[:, :, :], scalar=1.0, in1=iu[:, :, :],
                                                            op0=ALU.add, op1=ALU.mult))
                    own.wait()
                    dve.wait_ge(sqrt_ready, e + 1)
                    own.mark(nc.vector.tensor_tensor(iu[:, :, :], su[:, :, :], iu[:, :, :], ALU.mult))
                    own.wait()
                    for k in range(2):
                        own.mark(nc.vector.tensor_tensor_scan(out=yy[:, k, :], data0=aa[:, k, :], data1=iu[:, k, :], initial=0.0,
                                                              op0=ALU.mult, op1=ALU.add))
                    own.wait()
                    dve.wait_ge(gate_free, e + 1)
                    nc.vector.tensor_tensor(actl[:, :, :], yy[:, :, :], gg[:, :, :], ALU.mult).then_inc(act_ready, 1)
                for u in plan[0]:
                    split(u)
                if j < LRU_ITERS:
                    dve.wait_ge(gate_ready, STEP_LRU + j + 1)
                    if j:
                        dve.wait_ge(act_ready, STEP_LRU + j)
                    nc.vector.tensor_tensor(gg[:, :, :], two(GATE_BANK), sgate[:, :, :], ALU.mult).then_inc(gate_free, 1)
                for u in plan[1]:
                    split(u)
                if j:
                    dve.wait_ge(a_hi_ready, STEP_LRU + e + 1)
                    nc.vector.tensor_tensor(a_lo[:, e % 2, :, :], actl[:, :, :], a_hi[:, e % 2, :, :].bitcast(f32),
                                            ALU.subtract).then_inc(a_lo_ready, 1)
                for u in plan[2]:
                    split(u)
            residual(5, U_SC)

            normed("sc")
            turned("sc")
            for u in range(U_SC + 1, U_SC + 4):
                split(u)
            split(U_SC + 4, half=True)

            def sc_step(e, i=0, splits=3):
                g = GEN["sc"] + 2 * e
                dve.wait_ge(cg_ready, e + 1 + 2 * i)
                nc.vector.tensor_tensor(pp[:, :], ring[:, g % 4, S:2 * S], cgs[:, :], ALU.mult).then_inc(ring_free, 1)
                for k in range(splits):
                    if k == 1:
                        taps(e, i)
                    split(U_SC + 5 + 3 * e + k, i, half=sc_half(U_SC + 5 + 3 * e + k))
                if splits < 2:
                    taps(e, i)
                dve.wait_ge(a_hi_ready, STEP_SC + e + 1 + 2 * i)
                nc.vector.tensor_tensor(a_lo[:, e % 2, 0, :], acts[:, :], a_hi[:, e % 2, 0, :].bitcast(f32),
                                        ALU.subtract).then_inc(a_lo_ready, 1)

            def taps(e, i):
                g = GEN["sc"] + 2 * e
                c = C_SCONV + 3 * e + 6 * i
                dve.wait_ge(taps_ready, 2 * STEP_LRU + LRU_ITERS + e + 1 + 2 * i)
                own.mark(nc.vector.scalar_tensor_tensor(out=ct[:, 1:S], in0=pp[:, 0:S - 1], scalar=par[:, bass.ds(c + 1, 1)],
                                                        in1=ct[:, 1:S], op0=ALU.mult, op1=ALU.add))
                own.wait()
                own.mark(nc.vector.scalar_tensor_tensor(out=ct[:, 2:S], in0=pp[:, 0:S - 2], scalar=par[:, bass.ds(c, 1)],
                                                        in1=ct[:, 2:S], op0=ALU.mult, op1=ALU.add))
                own.wait()
                dve.wait_ge(gate_ready, STEP_SC + e + 1 + 2 * i)
                nc.vector.tensor_tensor(ys[:, :], ring[:, (g + 1) % 4, 0:S], ct[:, :], ALU.mult).then_inc(ring_free, 1)
                dve.wait_ge(ring_free, g + 2 + 4 * i)
                nc.vector.tensor_tensor(acts[:, :], ys[:, :], sgs[:, :], ALU.mult).then_inc(act_ready, 1)

            sc_step(0)
            with dve.Fori(0, (SC_ITERS - 4) // 2) as i:
                own.enter(4, i)
                for e in (1, 2):
                    sc_step(e, i)
            own.leave((SC_ITERS - 4) // 2)
            sc_step(SC_ITERS - 3)
            sc_step(SC_ITERS - 2, splits=1)
            sc_step(SC_ITERS - 1, splits=0)
            residual(6, UNITS)
            dve.wait_ge(rows_loaded, 32)
            for t in range(T):
                dve.wait_ge(rms_ready, RMS["final"] + t + 1)
                nc.vector.scalar_tensor_tensor(out=xn[:, t, :], in0=x[:, t, :], scalar=rstd[:, t:t + 1],
                                               in1=row[:, R_FINAL:R_FINAL + D], op0=ALU.mult, op1=ALU.mult).then_inc(out_ready, 1)

        @block.tensor
        def _(pe):
            PARTS = ((0, 0), (0, 1), (1, 0))
            h_parts, w_parts, a_parts = (h_hi, h_lo), (w_hi, w_lo), (a_hi, a_lo)

            def ready(u, i=0):
                pe.wait_ge(lo_split, u + 1 + RING * i)

            def bank(g, i=0):
                if g >= 4:
                    pe.wait_ge(ring_free, g - 3 + 4 * i)

            def turn(name, g0, f_hook=None):
                for t in range(T):
                    pe.wait_ge(xn_ready, XN[name] + t + 1)
                    for kc in range(KC):
                        g = g0 + kc // 2
                        if t == 0 and kc % 2 == 0:
                            bank(g)
                        lo = (kc % 2) * S + t * P
                        last = nc.tensor.transpose(ring[:, g % 4, lo:lo + P], xn[:, t, kc * P:(kc + 1) * P], ident[:, :])
                        if t == T - 1 and kc % 2 == 1:
                            last.then_inc(filled, 1)

            def wide(u, b, i=0, h_count=None, g=None, free=None):
                ready(u, i)
                if free is not None:
                    pe.wait_ge(*free)
                if g is not None:
                    bank(g, i)
                slot = u % RING
                for f in range(2):
                    for kc in range(KC):
                        if h_count is not None and f == 0 and kc % 2 == 0:
                            pe.wait_ge(ring_free, h_count + kc // 2 + 1)
                        for n, (a, c) in enumerate(PARTS):
                            lo = kc * 256 + f * P
                            last = nc.tensor.matmul(ring[:, b, f * S:(f + 1) * S], w_parts[a][:, slot, lo:lo + P],
                                                    h_parts[c][:, kc, :], start=kc == 0 and n == 0,
                                                    stop=kc == KC - 1 and n == 2, skip_group_check=True)
                last.then_inc(used, 1)

            def tall(u, lhs, kcs, first, end, i=0, layer_ends=False):
                ready(u, i)
                slot = u % RING
                for t in range(T):
                    for half in range(2):
                        for j, kc in enumerate(kcs):
                            for n, (a, c) in enumerate(PARTS):
                                last = nc.tensor.matmul(acc[:, t, half * 512:(half + 1) * 512], lhs(a, kc, t),
                                                        w_parts[c][:, slot, j * D + half * 512:j * D + (half + 1) * 512],
                                                        start=first and j == 0 and n == 0,
                                                        stop=end and j == len(kcs) - 1 and n == 2, skip_group_check=True)
                        if layer_ends and (t, half) != (T - 1, 1):
                            last.then_inc(bank_done, 1)
                last.then_inc(used, 1)

            def of_h(a, kc, t):
                return h_parts[a][:, kc, t * P:(t + 1) * P]

            def project(u0):
                for n in range(4):
                    tall(u0 + n, of_h, (2 * n, 2 * n + 1), first=n == 0, end=n == 3)

            def clear_acc():
                for t in range(T):
                    for half in range(2):
                        nc.tensor.matmul(acc[:, t, half * 512:(half + 1) * 512], zeros[:, 0:P], zeros[:, :],
                                         start=True, stop=False, skip_group_check=True)

            pe.wait_ge(made, 4)
            turn("mix0", GEN["norm_mix0"])
            pe.wait_ge(consts_loaded, 16 * N_CONSTS)
            g = GEN["rank"]
            bank(g)
            pe.wait_ge(wr_lo_ready, 1)
            for kc in range(KC):
                if kc % 2 == 0:
                    pe.wait_ge(ring_free, GEN["norm_mix0"] + kc // 2 + 1)
                for n, (a, c) in enumerate(PARTS):
                    last = nc.tensor.matmul(ring[0:2 * GLA_RANK, g % 4, 0:S], (wr_hi, wr_lo)[a][:, kc, :], h_parts[c][:, kc, :],
                                            start=kc == 0 and n == 0, stop=kc == KC - 1 and n == 2, skip_group_check=True)
            last.then_inc(filled, 1)
            for u, g in ((U_Q, GEN["q"]), (U_Q + 1, GEN["q"] + 1), (U_K, GEN["k"]), (U_K + 1, GEN["k"] + 1)):
                wide(u, g % 4, g=g)
            for d in range(2):
                for b in range(2):
                    g = GEN["z"] + 2 * d + b
                    bank(g)
                    for k in range(2):
                        h = 2 * b + k
                        last = nc.tensor.matmul(ring[:, g % 4, k * S:(k + 1) * S], gup[:, d, h * P:(h + 1) * P], rt[:, :],
                                                start=True, stop=True, skip_group_check=True)
                    last.then_inc(filled, 1)
            project(U_V)
            def scores(h):
                pe.wait_ge(prod_ready, h + 1)
                g = GEN["att"] + 2 * h
                bank(g)
                C = CHUNK
                for t in range(T):
                    lo = t * P
                    nc.tensor.matmul(ring[:, g % 4, lo:lo + P], ki[:, 0, lo:lo + P], qd[:, 0, lo:lo + P],
                                     start=True, stop=True, skip_group_check=True)
                    nc.tensor.matmul(ring[0:C, g % 4, lo + C:lo + P], kd[:, 0, lo:lo + C], qd[:, 0, lo + C:lo + P],
                                     start=True, stop=True, skip_group_check=True)
                    up = T * P + lo
                    nc.tensor.matmul(ring[:, g % 4, up:up + P], ki[:, 1, lo:lo + P], qd[:, 1, lo:lo + P],
                                     start=True, stop=True, skip_group_check=True)
                    last = nc.tensor.matmul(ring[C:P, g % 4, up:up + C], kd[:, 1, lo + C:lo + P], qd[:, 1, lo:lo + C],
                                            start=True, stop=True, skip_group_check=True)
                last.then_inc(filled, 1)
                bank(g + 1)
                for d in range(2):
                    last = nc.tensor.matmul(ring[:, (g + 1) % 4, d * P:(d + 1) * P], kt[:, d, :], qt[:, d, :],
                                            start=True, stop=True, skip_group_check=True)
                last.then_inc(filled, 1)

            for h in range(GLA_HEADS):
                scores(h)
                if h == 0:
                    pe.wait_ge(v_ready, T)
                tall(U_G + h, of_h, (2 * h, 2 * h + 1), first=h == 0, end=h == GLA_HEADS - 1)
            for t in range(T):
                pe.wait_ge(sg_ready, t + 1)
                for h in range(GLA_HEADS):
                    if t == 0:
                        pe.wait_ge(ring_free, GEN["att"] + 2 * h + 2)
                    at = slice(h * GLA_DV, (h + 1) * GLA_DV)
                    far = (1 - t) * P
                    nc.tensor.matmul(acc[:, t, at], qT[:, h, t * P:(t + 1) * P], v[:, t, at], start=True, stop=False,
                                     skip_group_check=True)
                    last = nc.tensor.matmul(acc[:, t, at], kT[:, h, far:far + P], v[:, 1 - t, at],
                                            start=False, stop=True, skip_group_check=True)
                    if h % 2 == 1:
                        last.then_inc(filled, 1)
            turn("gla", GEN["norm_turn"])
            for n in range(4):
                pe.wait_ge(ring_free, GEN["norm_turn"] + n + 1)
                tall(U_GO + n, of_h, (2 * n, 2 * n + 1), first=n == 0, end=n == 3, layer_ends=n == 3)

            def ffn(n):
                B, G, J = U_FFN[n], GEN[f"ffn{n}"], STEP_FFN[n]

                def up(e, i=0):
                    for k in range(2):
                        g = G + 2 * e + k
                        wide(up_unit(B, e, k), g % 4, i, g=g, h_count=GEN[f"norm_ffn{n}"] if e == 0 else None)

                def down(e, u, i=0, end=False):
                    pe.wait_ge(a_lo_ready, J + e + 1 + 2 * i)
                    tall(u, lambda a, kc, t: a_parts[a][:, e % 2, kc, t * P:(t + 1) * P], (0, 1), False, end, i, layer_ends=end)

                up(0)
                pe.wait_ge(acc_free[0], FREED[f"ffn{n}"])
                pe.wait_ge(acc_free[1], FREED[f"ffn{n}"])
                clear_acc()
                with pe.Fori(0, FFN_ITERS // 2) as i:
                    for e in (1, 2):
                        up(e, i)
                        down(e - 1, B + 3 * e + 1, i)
                down(FFN_ITERS - 1, B + FFN_UNITS - 1, end=True)

            turn("ffn0", GEN["norm_ffn0"])
            ffn(0)

            turn("mix1", GEN["norm_mix1"])
            for n in range(2):
                ready(U_KV + n)
                for j in range(4):
                    kc = 4 * n + j
                    if kc % 2 == 0:
                        pe.wait_ge(ring_free, GEN["norm_mix1"] + kc // 2 + 1)
                    for t in range(T):
                        g = GEN["kv"] + t
                        if kc == 0:
                            bank(g)
                        for m, (a, c) in enumerate(PARTS):
                            last = nc.tensor.matmul(ring[:, g % 4, :], of_h(a, kc, t), w_parts[c][:, (U_KV + n) % RING, j * 512:(j + 1) * 512],
                                                    start=kc == 0 and m == 0, stop=kc == KC - 1 and m == 2, skip_group_check=True)
                last.then_inc(used, 1)

            for t in range(T):
                for n in range(4):
                    ready(U_AQ + n)
                    for j in range(2):
                        kc = 2 * n + j
                        for half in range(2):
                            for m, (a, c) in enumerate(PARTS):
                                last = nc.tensor.matmul(acc[:, t, half * 512:(half + 1) * 512], of_h(a, kc, t),
                                                        w_parts[c][:, (U_AQ + n) % RING, j * D + half * 512:j * D + (half + 1) * 512],
                                                        start=kc == 0 and m == 0, stop=kc == KC - 1 and m == 2, skip_group_check=True)
                    if t == 0 and n == 3:
                        last.then_inc(q_tile, 1)
                    if t == 1:
                        last.then_inc(used, 1)
                    if (t, n) == (1, 0):
                        pe.wait_ge(roped, T)
                        bank(GEN["kT"])
                        for h in range(KV_HEADS):
                            for tile in range(T):
                                lo = h * S + tile * P
                                last = nc.tensor.transpose(ring[:, GEN["kT"] % 4, lo:lo + P], kr[:, tile, h * HD:(h + 1) * HD], ident[:, :])
                        last.then_inc(filled, 1)
            for t in range(T):
                for h in range(Q_HEADS):
                    if h % (Q_HEADS // 2) == 0:
                        pe.wait_ge(roped, T + 2 * t + 1 + 2 * h // Q_HEADS)
                    g = GEN["qT"] + h // 2
                    if t == 0 and h % 2 == 0:
                        bank(g)
                    lo = (h % 2) * S + t * P
                    last = nc.tensor.transpose(ring[:, g % 4, lo:lo + P], qr[:, t, h * HD:(h + 1) * HD], ident[:, :])
                    if t == T - 1 and h % 2 == 1:
                        last.then_inc(filled, 1)
            for h in range(Q_HEADS + 3):
                if h < Q_HEADS:
                    if h < 2:
                        pe.wait_ge(ring_free, GEN["qT"] + h + 1)
                    else:
                        pe.wait_ge(exp_ready, 2 * h - 2)
                    if h % 2 == 0:
                        pe.wait_ge(ring_free, GEN["qT"] + h // 2 + 1)
                    for t in range(T):
                        last = nc.tensor.matmul(ring[:, SCORE_BANKS[h % 2], t * S:(t + 1) * S], qT2[:, h, t * P:(t + 1) * P],
                                                kT2[:, h // GROUP, :], start=True, stop=True, skip_group_check=True)
                    last.then_inc(scores_ready, 1)
                e = h - 2
                if 0 <= e < Q_HEADS:
                    pe.wait_ge(probs_ready, e + 1)
                    if e < 2:
                        pe.wait_ge(ring_free, GEN["qT"] + 3 + e)
                    else:
                        pe.wait_ge(pt_ready, e - 1)
                    for t in range(T):
                        for kc in range(T):
                            lo = kc * S + t * P
                            last = nc.tensor.transpose(ring[:, TURNED_BANKS[e % 2], lo:lo + P], pm[:, e % 2, t, kc * P:(kc + 1) * P], ident[:, :])
                    last.then_inc(probs_turned, 1)
                e = h - 3
                if e >= 0:
                    pe.wait_ge(pt_ready, e + 1)
                    if e >= 2:
                        pe.wait_ge(o_free, e - 1)
                    else:
                        pe.wait_ge(acc_free[e], FREED["ao"])
                    first_v = KV_HEADS * HD + e // GROUP * HD
                    for kc in range(T):
                        last = nc.tensor.matmul(acc[:, 0, (e % 2) * 512:(e % 2) * 512 + S], kv[:, kc, first_v:first_v + HD],
                                                pt[:, e % 2, kc, :], start=kc == 0, stop=kc == T - 1, skip_group_check=True)
                    last.then_inc(o_ready, 1)
            for n in range(4):
                if n == 0:
                    pe.wait_ge(o_free, Q_HEADS)
                pe.wait_ge(o_free, 2 * n + 2)
                tall(U_AO + n, of_h, (2 * n, 2 * n + 1), first=n == 0, end=n == 3, layer_ends=n == 3)
            turn("ffn1", GEN["norm_ffn1"])
            ffn(1)

            turn("lru", GEN["norm_lru"])
            pe.wait_ge(gatew_loaded, 16)

            def gates(e):
                pe.wait_ge(conv_ready, e + 1)
                if e:
                    pe.wait_ge(ri_ready, 2 * e)
                for k in range(2):
                    for r in range(2):
                        last = nc.tensor.matmul(ring[:, HEAD_BANKS[k], r * S:(r + 1) * S],
                                                gatew[:, 2 * e + k, r * P:(r + 1) * P], xc[:, k, :],
                                                start=True, stop=True, skip_group_check=True)
                    last.then_inc(filled, 1)

            for j in range(LRU_ITERS + 2):
                if j < LRU_ITERS:
                    first = GEN["norm_lru"] if j == 0 else None
                    wide(LRU_UNIT["x", j], BRANCH_BANK, h_count=first, free=(branch_free, j) if j else (ring_free, GEN["norm_lru"] + 1))
                if 1 <= j < LRU_ITERS:
                    gates(j - 1)
                if j < LRU_ITERS:
                    wide(LRU_UNIT["g", j], GATE_BANK, free=(gate_free, j) if j else (ring_free, GEN["norm_lru"] + 2))
                if j == LRU_ITERS - 1:
                    gates(j)
                if j >= 2:
                    e = j - 2
                    pe.wait_ge(a_lo_ready, STEP_LRU + e + 1)
                    if e == 0:
                        for t in range(T):
                            pe.wait_ge(acc_free[t], FREED["lru"])
                    tall(LRU_UNIT["d", e], lambda a, kc, t: a_parts[a][:, e % 2, kc, t * P:(t + 1) * P], (0, 1),
                         first=e == 0, end=e == LRU_ITERS - 1, layer_ends=e == LRU_ITERS - 1)

            turn("sc", GEN["norm_sc"])

            def sc_up(e, i=0):
                for k in range(2):
                    g = GEN["sc"] + 2 * e + k
                    wide(up_unit(U_SC, e, k), g % 4, i, g=g, h_count=GEN["norm_sc"] if e == 0 else None)

            def sc_down(e, u, i=0, end=False):
                pe.wait_ge(a_lo_ready, STEP_SC + e + 1 + 2 * i)
                tall(u, lambda a, kc, t: a_parts[a][:, e % 2, 0, t * P:(t + 1) * P], (0,), False, end, i, layer_ends=end)

            sc_up(0)
            for t in range(T):
                pe.wait_ge(acc_free[t], FREED["sc"])
            clear_acc()
            with pe.Fori(0, (SC_ITERS - 2) // 2) as i:
                for e in (1, 2):
                    sc_up(e, i)
                    sc_down(e - 1, U_SC + 3 * e + 1, i)
            sc_up(SC_ITERS - 1)
            sc_down(SC_ITERS - 2, U_SC + 3 * (SC_ITERS - 1) + 1)
            sc_down(SC_ITERS - 1, UNITS - 1, end=True)


def wide_unit(w, columns):
    return w[:, columns].reshape(KC, P, 256).transpose(1, 0, 2).reshape(P, UNIT)


def tall_units(w, rows):
    made = w.reshape(-1, rows // P, P, w.shape[1]).transpose(0, 2, 1, 3).reshape(-1, P, rows // P * w.shape[1])
    return list(np.pad(made, ((0, 0), (0, 0), (0, UNIT - made.shape[2]))))


def tiles(a, n=P):
    return np.asarray(a).reshape(-1, n).T


def weight_stream(w):
    tile = lambda first, m: list(range(first + m * P, first + (m + 1) * P))
    units = []
    gla = w["gla_w_in"][0]
    for first in (0, GLA_KEYS):
        for n in range(2):
            units.append(wide_unit(gla, list(range(first + 256 * n, first + 256 * (n + 1)))))
    for first in (2 * GLA_KEYS, 2 * GLA_KEYS + D):
        units += tall_units(gla[:, first:first + D], 256)
    units += tall_units(w["gla_w_out"][0], 256)

    def ffn(n):
        up, down = w["ffn_w_up"][n], tall_units(w["ffn_w_down"][n], 256)
        for e in range(FFN_ITERS):
            for k in range(2):
                units.append(wide_unit(up, tile(0, 2 * e + k) + tile(D_FF, 2 * e + k)))
            if e:
                units.append(down[e - 1])
        units.append(down[-1])

    ffn(0)
    qkv = w["attn_w_qkv"][0]
    units.extend(tall_units(qkv[:, D:], 512))
    units.extend(tall_units(qkv[:, :D], 256))
    units.extend(tall_units(w["attn_w_out"][0], 256))
    ffn(1)
    lru_in, lru_down = w["a_w_in_2"][0], tall_units(w["a_w_out_2"][0], 256)
    lru = {}
    for e in range(LRU_ITERS):
        lru[LRU_UNIT["g", e]] = wide_unit(lru_in, list(range(256 * e, 256 * (e + 1))))
        lru[LRU_UNIT["x", e]] = wide_unit(lru_in, list(range(WIDTH + 256 * e, WIDTH + 256 * (e + 1))))
        lru[LRU_UNIT["d", e]] = lru_down[e]
    units += [lru[u] for u in range(U_LRU, U_SC)]
    sc_in, sc_down = w["b_w_in_2"][0], tall_units(w["b_w_out_2"][0], P)
    for e in range(SC_ITERS):
        units.append(wide_unit(sc_in, tile(WIDTH, e) + tile(2 * WIDTH, e)))
        units.append(wide_unit(sc_in, tile(0, e) + tile(3 * WIDTH, e)))
        if e:
            units.append(sc_down[e - 1])
    units.append(sc_down[-1])
    assert len(units) == UNITS
    return np.stack(units)


def channel_parameters(w):
    cols = [tiles(w["norm_mix"][0]), np.tile(tiles(w["gla_norm"][0]), (1, GLA_HEADS)), tiles(w["norm_ffn"][0]), tiles(w["norm_mix"][1]), tiles(w["norm_ffn"][1]),
            tiles(w["norm_g_2"][0]), tiles(w["norm_g_2"][1])]
    for n in range(2):
        taps = np.concatenate([w["ffn_w_conv"][n], w["ffn_b_conv"][n][None]])
        taps = taps.reshape(4, 2, D_FF // P, P).transpose(3, 2, 1, 0)
        cols.append(taps.reshape(P, -1))
    cols += [tiles(w["gla_b_gate_f"][0]), tiles(w["gla_b_gate_b"][0])]
    taps = np.concatenate([w["a_conv_w_2"][0], w["a_conv_b_2"][0][None]])
    cols.append(taps.reshape(5, LRU_HEADS, P).transpose(2, 1, 0).reshape(P, -1))
    cols.append(tiles(w["a_gate_b_2"][0]))
    cols.append(tiles(w["a_lambda_2"][0]))
    cols.append(w["b_conv_w_2"][0].reshape(3, SC_ITERS, P).transpose(2, 1, 0).reshape(P, -1))
    return np.ascontiguousarray(np.concatenate(cols, axis=1))


def rotation():
    grid, pairs = 64, HD // 4
    t = np.arange(S)
    inv = np.float32(10000.0) ** (-np.arange(pairs, dtype=np.float32) / np.float32(pairs))
    ang = np.concatenate([(t // grid).astype(np.float32)[:, None] * inv, (t % grid).astype(np.float32)[:, None] * inv], axis=1)
    cos, sin = np.cos(ang), np.sin(ang)
    both = np.stack([np.concatenate([cos, cos], axis=1), np.concatenate([-sin, sin], axis=1)], axis=1)
    return np.ascontiguousarray(both.reshape(T, P, 2, HD).transpose(1, 0, 2, 3).reshape(P, -1).astype(np.float32))


def kernel(**inputs):
    import concourse.bacc as bacc
    from concourse.bass_utils import run_bass_kernel_spmd

    w = {name: np.asarray(a) for name, a in inputs.items()}
    rank = w["gla_w_in"][0][:, 2 * GLA_KEYS + 2 * D:]
    gup = np.zeros((2, GLA_RANK, 2, GLA_KEYS), np.float32)
    gup[0, :, 0], gup[1, :, 1] = w["gla_w_gate_up_f"][0], w["gla_w_gate_up_b"][0]
    gate = w["a_gate_w_2"][0].transpose(1, 0, 2).reshape(P, -1)
    arrays = {
        "x": w["x"],
        "stream": weight_stream(w),
        "par": channel_parameters(w),
        "row": np.concatenate([w["final_g_2"], w["attn_q_norm"][0], w["attn_k_norm"][0]]),
        "wr": rank.reshape(KC, P, 2 * GLA_RANK).transpose(1, 0, 2).reshape(P, -1),
        "gup": gup.reshape(2 * GLA_RANK, -1),
        "gatew": gate,
        "rope": rotation(),
    }
    nc = bacc.Bacc("TRN2", target_bir_lowering=False, num_devices=1)
    sent, args = {}, []
    for name, a in arrays.items():
        a = np.ascontiguousarray(a)
        sent[f"in_{name}_dram"] = a
        args.append(nc.dram_tensor(f"in_{name}_dram", a.shape, mybir.dt.from_np(a.dtype), kind="ExternalInput").ap())
    out = nc.dram_tensor("out_dram", (1, S, D), mybir.dt.float32, kind="ExternalOutput").ap()
    two_block_kernel(nc, *args, out)
    r = run_bass_kernel_spmd(nc, [sent], core_ids=[0])
    return r.results[0]["out_dram"]
```
